# Optimizing a Trainium2 kernel written in Bass

```python
import jax, jax.numpy as jnp
from jax import lax
import numpy as np

D_MODEL = 1024
BATCH = 1
SEQ = 2048
DEPTH = 1

CHUNK = 64
RWKV_HEADS = 8
RWKV_HEAD_DIM = 64
RWKV_WIDTH = RWKV_HEADS * RWKV_HEAD_DIM
ATT_HEADS = 8
ATT_HEAD_DIM = 64
ATT_WIDTH = ATT_HEADS * ATT_HEAD_DIM
MIX_WIDTH = RWKV_WIDTH + ATT_WIDTH
DECAY_LORA = 64
AAA_LORA = 64
MV_LORA = 32
GATE_LORA = 128
RWKV_IN = 3 * RWKV_WIDTH + DECAY_LORA + AAA_LORA + GATE_LORA
RWKV_SPLITS = (RWKV_WIDTH, 2 * RWKV_WIDTH, 3 * RWKV_WIDTH,
               3 * RWKV_WIDTH + DECAY_LORA, 3 * RWKV_WIDTH + DECAY_LORA + AAA_LORA)
ATT_IN = 3 * ATT_WIDTH
IN_WIDTH = RWKV_IN + ATT_IN
PREV_CHUNKS = 8
BAND = (PREV_CHUNKS + 1) * CHUNK
REL_MAX = 256
REL_BUCKETS = REL_MAX + CHUNK
N_MEM = 256
XA_HEADS = 4
XA_HEAD_DIM = 128
XA_WIDTH = XA_HEADS * XA_HEAD_DIM
N_GROUPS = 4
EXPERTS_PER_GROUP = 8
N_EXPERTS = N_GROUPS * EXPERTS_PER_GROUP
TOP_K = 2
EXPERT_FF = 512
MOE_BLOCK = 128
NORM_EPS = 1e-6
LNX_EPS = 64e-5
NEG_INF = -1e30

kernel_name = 'hybrid_rwkv7_chunkattn_hmoe'

def rms_norm(x, g, eps=NORM_EPS):
    x32 = x.astype(jnp.float32)
    y = x32 * lax.rsqrt(jnp.mean(x32 * x32, axis=-1, keepdims=True) + eps)
    return (y * g.astype(jnp.float32)).astype(x.dtype)

def token_shift(u):
    return jnp.pad(u, ((0, 0), (1, 0), (0, 0)))[:, :-1]

def wkv7_scan(r, decay, k, v, a, b):
    B, S, H, N = r.shape

    def step(state, inp):
        r_t, w_t, k_t, v_t, a_t, b_t = inp
        sa = jnp.einsum('bhvk,bhk->bhv', state, a_t)
        state = (state * w_t[:, :, None, :] + sa[..., None] * b_t[:, :, None, :]
                 + v_t[..., None] * k_t[:, :, None, :])
        return state, jnp.einsum('bhvk,bhk->bhv', state, r_t)

    xs = tuple(jnp.moveaxis(t, 1, 0) for t in (r, decay, k, v, a, b))
    s0 = jnp.zeros((B, H, N, N), jnp.float32)
    _, ys = lax.scan(step, s0, xs)
    return jnp.moveaxis(ys, 0, 1)

def rwkv7_time_mix(u, v_first, mu, w0, w2, a0, a2, g2, k_k, k_a, r_k, lnx_w, lnx_b, vres):
    B, S, _ = u.shape
    H, N = RWKV_HEADS, RWKV_HEAD_DIM
    u = u.astype(jnp.float32)
    u = u + mu * (token_shift(u) - u)
    r, k, v, wl, al, gl = jnp.split(u, RWKV_SPLITS, axis=-1)
    w = w0 + jnp.tanh(wl) @ w2
    w = -jax.nn.softplus(-w) - 0.5
    decay = jnp.exp(-jnp.exp(w))
    a = jax.nn.sigmoid(a0 + al @ a2)
    g = jax.nn.sigmoid(gl) @ g2
    if vres is None:
        v_first = v
    else:
        v0, v1, v2 = vres
        v = v + (v_first - v) * jax.nn.sigmoid(v0 + (v @ v1) @ v2)
    kk = (k * k_k).reshape(B, S, H, N)
    kk = kk * lax.rsqrt(jnp.maximum(jnp.sum(kk * kk, axis=-1, keepdims=True), 1e-24))
    k = k * (1.0 + (a - 1.0) * k_a)
    r_h = r.reshape(B, S, H, N)
    k_h = k.reshape(B, S, H, N)
    v_h = v.reshape(B, S, H, N)
    a_h = a.reshape(B, S, H, N)
    y = wkv7_scan(r_h, decay.reshape(B, S, H, N), k_h, v_h, -kk, kk * a_h)
    mean = jnp.mean(y, axis=-1, keepdims=True)
    var = jnp.mean(jnp.square(y - mean), axis=-1, keepdims=True)
    y = ((y - mean) * lax.rsqrt(var + LNX_EPS)).reshape(B, S, RWKV_WIDTH) * lnx_w + lnx_b
    bonus = jnp.sum(r_h * k_h * r_k, axis=-1, keepdims=True) * v_h
    y = (y + bonus.reshape(B, S, RWKV_WIDTH)) * g
    return y, v_first

def rel_bias_band(table):
    q_off = jnp.arange(CHUNK)[:, None]
    k_off = jnp.arange(BAND)[None, :] - PREV_CHUNKS * CHUNK
    dist = jnp.clip(q_off - k_off, -(CHUNK - 1), REL_MAX) + (CHUNK - 1)
    return table[:, dist].astype(jnp.float32)

def chunk_band_attention(q, k, v, bias):
    B, S, H, Dh = q.shape
    nc = S // CHUNK
    pad = PREV_CHUNKS * CHUNK
    qc = q.reshape(B, nc, CHUNK, H, Dh).transpose(1, 0, 3, 2, 4)
    kp = jnp.pad(k, ((0, 0), (pad, 0), (0, 0), (0, 0))).transpose(0, 2, 1, 3)
    vp = jnp.pad(v, ((0, 0), (pad, 0), (0, 0), (0, 0))).transpose(0, 2, 1, 3)
    band_off = jnp.arange(BAND) - pad
    scale = Dh ** -0.5

    def one_chunk(args):
        c, qb = args
        start = c * CHUNK
        kb = lax.dynamic_slice_in_dim(kp, start, BAND, axis=2)
        vb = lax.dynamic_slice_in_dim(vp, start, BAND, axis=2)
        s = jnp.einsum('bhqd,bhkd->bhqk', qb.astype(jnp.float32), kb.astype(jnp.float32)) * scale + bias
        s = jnp.where((start + band_off) >= 0, s, NEG_INF)
        p = jax.nn.softmax(s, axis=-1)
        return jnp.einsum('bhqk,bhkd->bhqd', p.astype(vb.dtype), vb)

    out = lax.map(one_chunk, (jnp.arange(nc, dtype=jnp.int32), qc))
    return out.transpose(1, 0, 3, 2, 4).reshape(B, S, H * Dh)

def memory_cross_attention(h, mem_n, w_q, w_kv, w_o, q_norm, k_norm):
    B, S, _ = h.shape
    M = mem_n.shape[1]
    q = (h @ w_q).reshape(B, S, XA_HEADS, XA_HEAD_DIM)
    k, v = jnp.split(mem_n @ w_kv, 2, axis=-1)
    k = k.reshape(B, M, XA_HEADS, XA_HEAD_DIM)
    v = v.reshape(B, M, XA_HEADS, XA_HEAD_DIM)
    q = rms_norm(q, q_norm)
    k = rms_norm(k, k_norm)
    s = jnp.einsum('bshd,bmhd->bhsm', q.astype(jnp.float32), k.astype(jnp.float32)) * (XA_HEAD_DIM ** -0.5)
    p = jax.nn.softmax(s, axis=-1)
    o = jnp.einsum('bhsm,bmhd->bshd', p.astype(v.dtype), v).reshape(B, S, XA_WIDTH)
    return o @ w_o

def hierarchical_moe(h, w_group, b_group, w_route, b_route, w_gate, w_up, w_down):
    B, S, D = h.shape
    T = B * S
    xt = h.reshape(T, D)
    group_p = jax.nn.softmax((xt @ w_group).astype(jnp.float32) + b_group, axis=-1)
    g_top = jnp.argmax(group_p, axis=-1).astype(jnp.int32)
    g_gate = jnp.take_along_axis(group_p, g_top[:, None], axis=-1)[:, 0]
    logits = ((xt @ w_route).astype(jnp.float32) + b_route).reshape(T, N_GROUPS, EXPERTS_PER_GROUP)
    logits = jnp.take_along_axis(logits, g_top[:, None, None], axis=1)[:, 0]
    p_in = jax.nn.softmax(logits, axis=-1)
    top_p, top_j = lax.top_k(p_in, TOP_K)
    top_p = top_p / jnp.sum(top_p, axis=-1, keepdims=True)
    weights = g_gate[:, None] * top_p
    expert_id = g_top[:, None] * EXPERTS_PER_GROUP + top_j.astype(jnp.int32)
    A = T * TOP_K
    e = expert_id.reshape(A)
    tok = jnp.repeat(jnp.arange(T, dtype=jnp.int32), TOP_K)
    wts = weights.reshape(A)
    order = jnp.argsort(e)
    e_s, tok_s, w_s = e[order], tok[order], wts[order]
    counts = jnp.bincount(e, length=N_EXPERTS)
    starts = jnp.cumsum(counts) - counts
    padded = ((counts + MOE_BLOCK - 1) // MOE_BLOCK) * MOE_BLOCK
    pends = jnp.cumsum(padded)
    pstarts = pends - padded
    dest = pstarts[e_s] + (jnp.arange(A, dtype=jnp.int32) - starts[e_s])
    n_blocks = (A + N_EXPERTS * (MOE_BLOCK - 1) + MOE_BLOCK - 1) // MOE_BLOCK
    L = n_blocks * MOE_BLOCK
    buf_tok = jnp.full((L,), T, jnp.int32).at[dest].set(tok_s)
    buf_w = jnp.zeros((L,), wts.dtype).at[dest].set(w_s)
    block_expert = jnp.minimum(
        jnp.searchsorted(pends, jnp.arange(n_blocks) * MOE_BLOCK, side='right'), N_EXPERTS - 1).astype(jnp.int32)
    xs = jnp.concatenate([xt, jnp.zeros((1, D), xt.dtype)], axis=0)[buf_tok].reshape(n_blocks, MOE_BLOCK, D)

    def expert_block(args):
        xb, eid = args
        return (jax.nn.silu(xb @ w_gate[eid]) * (xb @ w_up[eid])) @ w_down[eid]

    yb = lax.map(expert_block, (xs, block_expert)).reshape(L, D)
    out = jnp.zeros((T + 1, D), yb.dtype).at[buf_tok].add(yb * buf_w[:, None].astype(yb.dtype))
    return out[:T].reshape(B, S, D)

def setup_inputs(seed: int = 0) -> dict:
    key = jax.random.key(seed)
    ks = iter(jax.random.split(key, 48))

    def nrm(shape, scale):
        return jax.random.normal(next(ks), shape, jnp.float32) * scale

    L, LV, D = DEPTH, DEPTH - 1, D_MODEL
    return {
        'x': nrm((BATCH, SEQ, D), 1.0),
        'mem': nrm((BATCH, N_MEM, D), 1.0),
        'norm_mix': 1.0 + nrm((L, D), 0.02),
        'w_in': nrm((L, D, IN_WIDTH), D ** -0.5),
        'shift_mu': jax.random.uniform(next(ks), (L, RWKV_IN), jnp.float32),
        'decay_w0': jax.random.uniform(next(ks), (L, RWKV_WIDTH), jnp.float32, -6.0, -1.0),
        'decay_w2': nrm((L, DECAY_LORA, RWKV_WIDTH), 0.1),
        'iclr_a0': nrm((L, RWKV_WIDTH), 0.1),
        'iclr_a2': nrm((L, AAA_LORA, RWKV_WIDTH), 0.1),
        'gate_g2': nrm((L, GATE_LORA, RWKV_WIDTH), GATE_LORA ** -0.5),
        'rw_k_k': 0.85 + nrm((L, RWKV_WIDTH), 0.05),
        'rw_k_a': 1.0 + nrm((L, RWKV_WIDTH), 0.05),
        'rw_r_k': nrm((L, RWKV_HEADS, RWKV_HEAD_DIM), 0.1),
        'lnx_w': 1.0 + nrm((L, RWKV_WIDTH), 0.05),
        'lnx_b': nrm((L, RWKV_WIDTH), 0.01),
        'vres_v0': 1.0 + nrm((LV, RWKV_WIDTH), 0.1),
        'vres_v1': nrm((LV, RWKV_WIDTH, MV_LORA), RWKV_WIDTH ** -0.5),
        'vres_v2': nrm((LV, MV_LORA, RWKV_WIDTH), 0.1),
        'att_q_norm': 1.0 + nrm((L, ATT_HEAD_DIM), 0.02),
        'att_k_norm': 1.0 + nrm((L, ATT_HEAD_DIM), 0.02),
        'att_rel_bias': nrm((L, ATT_HEADS, REL_BUCKETS), 0.5),
        'att_out_norm': 1.0 + nrm((L, ATT_WIDTH), 0.02),
        'w_out': nrm((L, MIX_WIDTH, D), 0.5 * MIX_WIDTH ** -0.5),
        'norm_xa': 1.0 + nrm((L, D), 0.02),
        'norm_mem': 1.0 + nrm((L, D), 0.02),
        'xa_w_q': nrm((L, D, XA_WIDTH), D ** -0.5),
        'xa_w_kv': nrm((L, D, 2 * XA_WIDTH), D ** -0.5),
        'xa_w_o': nrm((L, XA_WIDTH, D), 0.5 * XA_WIDTH ** -0.5),
        'xa_q_norm': 1.0 + nrm((L, XA_HEAD_DIM), 0.02),
        'xa_k_norm': 1.0 + nrm((L, XA_HEAD_DIM), 0.02),
        'norm_ffn': 1.0 + nrm((L, D), 0.02),
        'moe_w_group': nrm((L, D, N_GROUPS), D ** -0.5),
        'moe_b_group': nrm((L, N_GROUPS), 0.01),
        'moe_w_route': nrm((L, D, N_EXPERTS), D ** -0.5),
        'moe_b_route': nrm((L, N_EXPERTS), 0.01),
        'moe_w_gate': nrm((L, N_EXPERTS, D, EXPERT_FF), D ** -0.5),
        'moe_w_up': nrm((L, N_EXPERTS, D, EXPERT_FF), D ** -0.5),
        'moe_w_down': nrm((L, N_EXPERTS, EXPERT_FF, D), 0.5 * EXPERT_FF ** -0.5),
    }

def reference(x, mem, norm_mix, w_in, shift_mu, decay_w0, decay_w2, iclr_a0, iclr_a2, gate_g2,
              rw_k_k, rw_k_a, rw_r_k, lnx_w, lnx_b, vres_v0, vres_v1, vres_v2,
              att_q_norm, att_k_norm, att_rel_bias, att_out_norm, w_out,
              norm_xa, norm_mem, xa_w_q, xa_w_kv, xa_w_o, xa_q_norm, xa_k_norm,
              norm_ffn, moe_w_group, moe_b_group, moe_w_route, moe_b_route,
              moe_w_gate, moe_w_up, moe_w_down):
    B, S, _ = x.shape
    v_first = None
    for l in range(DEPTH):
        h = rms_norm(x, norm_mix[l])
        proj = h @ w_in[l]
        vres = None if l == 0 else (vres_v0[l - 1], vres_v1[l - 1], vres_v2[l - 1])
        y_r, v_first = rwkv7_time_mix(proj[..., :RWKV_IN], v_first, shift_mu[l], decay_w0[l], decay_w2[l],
                                      iclr_a0[l], iclr_a2[l], gate_g2[l], rw_k_k[l], rw_k_a[l], rw_r_k[l],
                                      lnx_w[l], lnx_b[l], vres)
        q, k, v = jnp.split(proj[..., RWKV_IN:], 3, axis=-1)
        q = rms_norm(q.reshape(B, S, ATT_HEADS, ATT_HEAD_DIM), att_q_norm[l])
        k = rms_norm(k.reshape(B, S, ATT_HEADS, ATT_HEAD_DIM), att_k_norm[l])
        v = v.reshape(B, S, ATT_HEADS, ATT_HEAD_DIM)
        y_a = chunk_band_attention(q, k, v, rel_bias_band(att_rel_bias[l]))
        y_a = rms_norm(y_a, att_out_norm[l])
        x = x + jnp.concatenate([y_r.astype(x.dtype), y_a.astype(x.dtype)], axis=-1) @ w_out[l]
        x = x + memory_cross_attention(rms_norm(x, norm_xa[l]), rms_norm(mem, norm_mem[l]),
                                       xa_w_q[l], xa_w_kv[l], xa_w_o[l], xa_q_norm[l], xa_k_norm[l])
        x = x + hierarchical_moe(rms_norm(x, norm_ffn[l]), moe_w_group[l], moe_b_group[l], moe_w_route[l],
                                 moe_b_route[l], moe_w_gate[l], moe_w_up[l], moe_w_down[l])
    return x


_drawn_inputs = setup_inputs


def setup_inputs(seed=0):
    import zlib

    import numpy as np

    out = dict(_drawn_inputs(seed))
    spreads = {}
    factors = {'norm_mix': 3.147,
     'decay_w2': 5.775,
     'iclr_a0': 5.336,
     'rw_k_k': 4.108,
     'rw_k_a': 4.329,
     'lnx_w': 4.222,
     'lnx_b': 8.0,
     'att_q_norm': 5.466,
     'att_k_norm': 5.207,
     'att_out_norm': 5.127,
     'norm_xa': 8.0,
     'norm_mem': 8.0,
     'xa_q_norm': 8.0,
     'xa_k_norm': 8.0,
     'norm_ffn': 3.965,
     'moe_b_group': 8.0,
     'moe_b_route': 6.673}
    for name, (base, spread) in spreads.items():
        noise = np.random.default_rng([zlib.crc32(name.encode()), seed]).standard_normal(out[name].shape)
        drawn = base * np.exp(spread * noise) if base else spread * noise
        out[name] = __import__('jax').numpy.asarray(drawn.astype(out[name].dtype))
    for name, factor in factors.items():
        out[name] = (out[name] * factor).astype(out[name].dtype)
    return out
```

```python
from contextlib import ExitStack

import numpy as np

import concourse.bass as bass
from concourse import mybir
from concourse.alu_op_type import AluOpType as ALU

F32 = mybir.dt.float32
I32 = mybir.dt.int32
ACT = mybir.ActivationFunctionType
AX = mybir.AxisListType

P = 128
SEQ, DM = 2048, 1024
TILES = SEQ // P
KT = DM // P
CHUNK, HD, HEADS = 64, 64, 8
RW = HEADS * HD
CT = RW // P
LORA, GATE = 64, 128
RW_IN = 3 * RW + 2 * LORA + GATE
RW_TILES = RW_IN // P
IN_WIDTH = RW_IN + 3 * RW
PREV = 8 * CHUNK
BAND = PREV + P
KB = BAND // P
N_MEM, XH, XD = 256, 4, 128
XW = XH * XD
MT = N_MEM // P
GROUPS, PER_GROUP, FF = 4, 8, 512
EXPERTS = GROUPS * PER_GROUP
LOGITS = GROUPS + EXPERTS
FT = FF // P
BLOCKS = (2 * SEQ + EXPERTS * (P - 1)) // P + 1
SLOTS = BLOCKS * P
N512 = 512
EPS, LNX_EPS = 1e-6, 64e-5
NEG = -1e30
HALF_E = float(np.exp(-0.5) / 2)
REL_MAX = 256


class Signals:

    def __init__(self, nc, stack, stage, turns="", dma_turns=""):
        self.nc, self.stage, self.made = nc, stage, {}
        stack.callback(self.clear)
        for names, one in ((turns, 1), (dma_turns, 16)):
            for name in names.split():
                nc.gpsimd.sem_inc(self(name), one)

    def __call__(self, name):
        if name not in self.made:
            self.made[name] = self.nc.alloc_semaphore(f"{self.stage}_{name}")
        return self.made[name]

    def clear(self):
        self.nc.clear_and_free_semaphores(list(self.made.values()))
        self.nc.all_engine_barrier()


class Memory:

    def __init__(self, nc, stack, stage):
        self.nc, self.stack, self.stage = nc, stack, stage

    def __call__(self, name, *shape, dt=F32):
        return self.stack.enter_context(self.nc.sbuf_tensor(f"{self.stage}_{name}", list(shape), dt))


def column(vector, tiles):
    return vector.rearrange("(c p) -> p c", c=tiles)


def spread(ap, n):
    return ap.unsqueeze(2).broadcast_to([ap.shape[0], ap.shape[1], n])


def per_head(ap, n):
    return ap.unsqueeze(1).broadcast_to([ap.shape[0], n, ap.shape[1]])


def build_constants(nc, c):
    with ExitStack() as stack:
        sem = Signals(nc, stack, "constant")
        block = stack.enter_context(nc.Block())

        @block.gpsimd
        def _(pool):
            made = [0]

            def then(instruction):
                instruction.then_inc(sem("constants"), 1)
                made[0] += 1
                pool.wait_ge(sem("constants"), made[0])

            then(pool.memset(c.eps[:], EPS))
            then(pool.memset(c.lnx_eps[:], LNX_EPS))
            then(pool.memset(c.ones[:], 1.0))
            then(pool.memset(c.every[:], 1.0))
            then(pool.memset(c.ident[:], 0.0))
            then(pool.affine_select(out=c.ident[:], in_=c.ident[:], compare_op=ALU.not_equal, fill=1.0, base=0,
                                    pattern=[[-1, P]], channel_multiplier=1))


def build_masks(pool, c, sem):
    made = [0]

    def then(instruction):
        instruction.then_inc(sem("masks"), 1)
        made[0] += 1
        pool.wait_ge(sem("masks"), made[0])

    def keep(out, pattern, base, channel, compare, fill=0.0):
        then(pool.affine_select(out=out, in_=out, compare_op=compare, fill=fill, base=base, pattern=pattern,
                                channel_multiplier=channel))

    for h in range(2):
        then(pool.memset(c.same_head[:, h * HD:(h + 1) * HD], 1.0))
    keep(c.same_head[:, 0:HD], [[0, HD]], HD - 1, -1, ALU.is_ge)
    keep(c.same_head[:, HD:P], [[0, HD]], -HD, 1, ALU.is_ge)
    then(pool.memset(c.all_heads[:], 1.0))
    for t in range(CT):
        keep(c.all_heads[:, t, :], [[-HD, HEADS]], P * t, 1, ALU.is_ge)
        keep(c.all_heads[:, t, :], [[HD, HEADS]], HD - 1 - P * t, -1, ALU.is_ge)
    then(pool.memset(c.head_rows[:], 1.0))
    keep(c.head_rows[:], [[1, RW]], 0, -HD, ALU.is_ge)
    keep(c.head_rows[:], [[-1, RW]], HD - 1, HD, ALU.is_ge)
    for half in range(2):
        rows = slice(half * HD, half * HD + HD)
        then(pool.memset(c.causal[rows], 1.0))
        keep(c.causal[rows, 0:HD], [[1, HD]], -1, -1, ALU.is_ge)
        keep(c.causal[rows, HD:P], [[1, HD]], 0, -1, ALU.is_ge)
        then(pool.memset(c.ident_half[rows], 0.0))
        keep(c.ident_half[rows], [[-1, HD]], 0, 1, ALU.not_equal, fill=1.0)
    for n, m in enumerate(LEVELS):
        for half in range(2):
            rows = slice(half * HD, half * HD + HD)
            view = c.level_mask[rows, n, :].rearrange("p (b x) -> p b x", x=2 * m)
            then(pool.memset(view, 1.0))
            b = HD // (2 * m)
            keep(view, [[-2 * m, b], [0, 2 * m]], -m, 1, ALU.is_ge)
            keep(view, [[2 * m, b], [0, 2 * m]], 2 * m - 1, -1, ALU.is_ge)
            keep(view, [[0, b], [-1, 2 * m]], m - 1, 0, ALU.is_ge)
            if m == 1:
                view = c.level_mask_t[rows, n, :].rearrange("p (b x) -> p b x", x=2 * m)
                then(pool.memset(view, 1.0))
                keep(view, [[-2 * m, b], [0, 2 * m]], 0, 1, ALU.is_ge)
                keep(view, [[2 * m, b], [0, 2 * m]], m - 1, -1, ALU.is_ge)
                keep(view, [[0, b], [1, 2 * m]], -m, 0, ALU.is_ge)
    then(pool.memset(c.within[:], 1.0))
    then(pool.memset(c.within[:].rearrange("p (n x) -> p n x", x=CHUNK)[:, :, 0:1], 0.0))


LEVELS = (1, 2, 4, 8, 16, 32)


def norm_and_project_v(nc, a, c, dram, banks):
    with ExitStack() as stack:
        sb = Memory(nc, stack, "norm")
        both = lambda *names: " ".join(f"{n}{half}" for n in names for half in range(2))
        sem = Signals(nc, stack, "norm", both("squared", "log_square", "rstd", "x_scaled", "turned", "h_now", "h_kept",
                                      "v_done", "v_copied"), both("x_in", "v_out"))
        x_in = [sb(f"x_in{i}", P, DM) for i in range(2)]
        x_n = [sb(f"x_n{i}", P, DM) for i in range(2)]
        squares = [sb(f"squares{i}", P, DM) for i in range(2)]
        square_sum = [sb(f"square_sum{i}", P, 1) for i in range(2)]
        log_square = [sb(f"log_square{i}", P, 1) for i in range(2)]
        rstd = [sb(f"rstd{i}", P, 1) for i in range(2)]
        h_now = [sb(f"h_now{i}", P, KT, P) for i in range(2)]
        w_v = sb("w_v", P, KT, RW)
        v_out = [sb(f"v_out{i}", P, RW) for i in range(2)]
        gain = sb("gain_mix", P, KT)
        turned = [banks[:, 0:2], banks[:, 3:5]]
        v_ps = [banks[:, 2], banks[:, 5]]
        block = stack.enter_context(nc.Block())
        x_tiles = a["x"].rearrange("b (t p) d -> (b t) p d", p=P)

        @block.sync
        def _(sp):
            with nc.allow_non_contiguous_dma(reason="a gain vector over partitions"):
                sp.dma_start(gain[:], column(a["norm_mix"][0], KT)).then_inc(sem("gain_in"), 16)
            v_col = RW_IN + 2 * RW
            sp.dma_start(w_v[:], a["w_in"][0, :, v_col:v_col + RW].rearrange("(k p) n -> p k n", p=P)).then_inc(
                sem("w_v_in"), 16)
            sp.wait_ge(sem("zeros_set"), 1)
            for k in range(PREV // P):
                sp.dma_start(dram["v"][k * P:(k + 1) * P, :], squares[0][:, 0:RW]).then_inc(sem("pads_out"), 16)
            for k in range(CT):
                sp.dma_start(dram["k"][k, :, 0:PREV], squares[0][:, 0:PREV]).then_inc(sem("pads_out"), 16)
            with sp.Fori(0, TILES // 2) as i:
                for half in range(2):
                    sp.wait_ge(sem(f"x_scaled{half}"), i + 1)
                    sp.wait_ge(sem(f"squared{half}"), i + 1)
                    sp.dma_start(x_in[half][:], x_tiles[bass.ds(2 * i + half, 1)].rearrange(
                        "o p d -> (o p) d")).then_inc(sem(f"x_in{half}"), 16)
            for half in range(2):
                sp.wait_ge(sem(f"v_out{half}"), 16 * (TILES // 2 + 1))

        @block.gpsimd
        def _(pool):
            pool.memset(squares[0][:], 0.0).then_inc(sem("zeros_set"), 1)
            build_masks(pool, c, sem)

        @block.scalar
        def _(act):
            act.preload_act_table_set("natural_log_exp_and_others")
            act.wait_ge(sem("pads_out"), 16 * (PREV // P + CT))
            with act.Fori(0, TILES // 2) as i:
                for half in range(2):
                    act.wait_ge(sem(f"log_square{half}"), i + 1)
                    act.wait_ge(sem(f"x_in{half}"), 16 * i + 32)
                    act.activation(squares[half][:], x_in[half][:], ACT.Square, accum_out=square_sum[half][:]).then_inc(
                        sem(f"squared{half}"), 1)
                    act.wait_ge(sem(f"squared{half}"), i + 2)
                    act.activation(log_square[half][:], square_sum[half][:], ACT.Ln, scale=1.0 / DM,
                                   bias=c.eps[:, 0:1]).then_inc(sem(f"log_square{half}"), 1)
                    act.wait_ge(sem(f"x_scaled{half}"), i + 1)
                    act.wait_ge(sem(f"log_square{half}"), i + 2)
                    act.activation(rstd[half][:], log_square[half][:], ACT.Exp, scale=-0.5).then_inc(
                        sem(f"rstd{half}"), 1)
                for half in range(2):
                    act.wait_ge(sem(f"h_now{half}"), i + 2)
                    act.copy(c.h_t[:, :, bass.ds((2 * i + half) * P, P)], h_now[half][:]).then_inc(
                        sem(f"h_kept{half}"), 1)
                    act.wait_ge(sem(f"v_out{half}"), 16 * i + 16)
                    act.wait_ge(sem(f"v_done{half}"), i + 2)
                    act.copy(v_out[half][:], v_ps[half]).then_inc(sem(f"v_copied{half}"), 1)
                    act.wait_ge(sem(f"v_copied{half}"), i + 2)
                    act.dma_start(dram["v"][bass.ds((2 * i + half) * P + PREV, P), :], v_out[half][:]).then_inc(
                        sem(f"v_out{half}"), 16)

        @block.vector
        def _(dve):
            dve.wait_ge(sem("gain_in"), 16)
            with dve.Fori(0, TILES // 2) as i:
                for half in range(2):
                    dve.wait_ge(sem(f"turned{half}"), i + 1)
                    dve.wait_ge(sem(f"x_in{half}"), 16 * i + 32)
                    dve.wait_ge(sem(f"rstd{half}"), i + 2)
                    dve.tensor_scalar(x_n[half][:], x_in[half][:], rstd[half][:, 0:1], None, ALU.mult).then_inc(
                        sem(f"x_scaled{half}"), 1)
                for half in range(2):
                    dve.wait_ge(sem(f"h_kept{half}"), i + 1)
                    dve.wait_ge(sem(f"v_done{half}"), i + 1)
                    dve.wait_ge(sem(f"turned{half}"), i + 2)
                    dve.tensor_tensor(h_now[half][:], turned[half].rearrange("p b (k t) -> p (b k) t", t=P),
                                      spread(gain[:], P), ALU.mult).then_inc(sem(f"h_now{half}"), 1)

        @block.tensor
        def _(pe):
            pe.wait_ge(sem("w_v_in"), 16)
            with pe.Fori(0, TILES // 2) as i:
                for half in range(2):
                    pe.wait_ge(sem(f"h_now{half}"), i + 1)
                    pe.wait_ge(sem(f"x_scaled{half}"), i + 2)
                    for k in range(KT):
                        last = pe.transpose(turned[half][:, k // 4, (k % 4) * P:(k % 4 + 1) * P],
                                            x_n[half][:, k * P:(k + 1) * P], c.ident[:])
                    last.then_inc(sem(f"turned{half}"), 1)
                for half in range(2):
                    pe.wait_ge(sem(f"v_copied{half}"), i + 1)
                    pe.wait_ge(sem(f"h_now{half}"), i + 2)
                    for k in range(KT):
                        last = pe.matmul(v_ps[half], h_now[half][:, k, :], w_v[:, k, :], start=k == 0,
                                         stop=k == KT - 1)
                    last.then_inc(sem(f"v_done{half}"), 1)


def project_rwkv(nc, a, c, dram, banks):
    with ExitStack() as stack:
        sb = Memory(nc, stack, "rwkv")
        names = [f"{n}{half}" for n in ("u_done", "difference", "mixed") for half in range(2)]
        names += [f"{n}{half}_{q}" for n in ("product", "copied") for half in range(2) for q in range(4)]
        sem = Signals(nc, stack, "rwkv", " ".join(names), "mixed_out0 mixed_out1")
        w = [sb(f"w_tile{i}", P, KT, P) for i in range(2)]
        u = [sb(f"u{i}", P, SEQ + 1) for i in range(2)]
        difference = sb("difference", P, SEQ)
        mixed = [sb(f"mixed{i}", P, SEQ) for i in range(2)]
        mu = sb("mu", P, RW_TILES)
        block = stack.enter_context(nc.Block())
        w_tiles = a["w_in"][0].rearrange("(k p) n -> p k n", p=P)

        @block.sync
        def _(sp):
            with nc.allow_non_contiguous_dma(reason="the shift's weights over partitions"):
                sp.dma_start(mu[:], column(a["shift_mu"][0], RW_TILES)).then_inc(sem("mu_in"), 16)
            with sp.Fori(0, RW_TILES // 2) as i:
                for half in range(2):
                    sp.wait_ge(sem(f"mixed{half}"), i + 2)
                    sp.dma_start(dram["rw"][bass.ds(2 * i + half, 1)].rearrange("o p n -> (o p) n"),
                                 mixed[half][:]).then_inc(sem(f"mixed_out{half}"), 16)
            for half in range(2):
                sp.wait_ge(sem(f"mixed_out{half}"), 16 * (RW_TILES // 2 + 1))

        @block.tensor
        def _(pe):
            with pe.Fori(0, RW_TILES // 2) as i:
                for half in range(2):
                    pe.wait_ge(sem(f"w_in{half}"), 16 * i + 16)
                    for q in range(4):
                        pe.wait_ge(sem(f"copied{half}_{q}"), i + 1)
                        for k in range(KT):
                            last = pe.matmul(banks[:, 4 * half + q], w[half][:, k, :],
                                             c.h_t[:, k, q * N512:(q + 1) * N512], start=k == 0, stop=k == KT - 1)
                        last.then_inc(sem(f"product{half}_{q}"), 1)

        @block.scalar
        def _(act):
            for half in range(2):
                act.dma_start(w[half][:], w_tiles[:, :, half * P:(half + 1) * P]).then_inc(sem(f"w_in{half}"), 16)
                act.activation(u[half][:, 0:1], c.ones[:, 0:1], ACT.Copy, scale=0.0).then_inc(sem("first_set"), 1)
            with act.Fori(0, RW_TILES // 2) as i:
                for half in range(2):
                    act.wait_ge(sem(f"mixed{half}"), i + 1)
                    for q in range(4):
                        act.wait_ge(sem(f"product{half}_{q}"), i + 2)
                        act.copy(u[half][:, 1 + q * N512:1 + (q + 1) * N512], banks[:, 4 * half + q]).then_inc(
                            sem(f"copied{half}_{q}"), 1)
                    act.dma_start(w[half][:], w_tiles[:, :, bass.ds((2 * i + 2 + half) * P, P)]).then_inc(
                        sem(f"w_in{half}"), 16)
            for half in range(2):
                act.wait_ge(sem(f"w_in{half}"), 16 * (RW_TILES // 2 + 1))

        @block.vector
        def _(dve):
            dve.wait_ge(sem("mu_in"), 16)
            dve.wait_ge(sem("first_set"), 2)
            with dve.Fori(0, RW_TILES // 2) as i:
                for half in range(2):
                    dve.wait_ge(sem(f"mixed{1 - half}"), i + 1 + half)
                    for q in range(4):
                        dve.wait_ge(sem(f"copied{half}_{q}"), i + 2)
                    dve.tensor_tensor(difference[:], u[half][:, 0:SEQ], u[half][:, 1:SEQ + 1],
                                      ALU.subtract).then_inc(sem(f"difference{half}"), 1)
                    dve.wait_ge(sem(f"mixed_out{half}"), 16 * i + 16)
                    dve.wait_ge(sem(f"difference{half}"), i + 2)
                    dve.scalar_tensor_tensor(out=mixed[half][:], in0=difference[:], scalar=mu[:, bass.ds(2 * i + half, 1)],
                                             in1=u[half][:, 1:SEQ + 1], op0=ALU.mult, op1=ALU.add).then_inc(
                        sem(f"mixed{half}"), 1)


def project_attention(nc, a, c, m, dram, banks):
    with ExitStack() as stack:
        sb = Memory(nc, stack, "attention")
        pairs = [f"{half}_{q}" for half in range(2) for q in range(4)]
        names = [n + p for n in ("product", "copied", "squared", "summed", "logged", "rstd", "widened", "normed")
                 for p in pairs]
        sem = Signals(nc, stack, "attention", " ".join(names), "out0 out1")
        w = [sb(f"w_tile{i}", P, KT, P) for i in range(2)]
        u = sb("u", P, 4, N512)
        square = sb("square", P, 4, N512)
        logged = sb("logged", 2, 4, N512)
        rstd = sb("rstd", 2, 4, N512)
        normed = [sb(f"normed{i}", P, 4, N512) for i in range(2)]
        gain = sb("gain", P, 2)
        block = stack.enter_context(nc.Block())
        w_tiles = a["w_in"][0].rearrange("(k p) n -> p k n", p=P)
        outs = [dram["q"][:, :, 0:SEQ], dram["k"][:, :, PREV:PREV + SEQ]]

        @block.sync
        def _(sp):
            with nc.allow_non_contiguous_dma(reason="gain vectors over partitions"):
                for half, name in enumerate(("att_q_norm", "att_k_norm")):
                    for h in range(2):
                        sp.dma_start(gain[h * HD:(h + 1) * HD, half:half + 1], column(a[name][0], 1)).then_inc(
                            sem("gain_in"), 16)
            for tile, name in ((m.w_out, "w_out"), (m.w_q, "xa_w_q"), (m.w_o, "xa_w_o")):
                sp.dma_start(tile[:], a[name][0].rearrange("(k p) n -> p k n", p=P)).then_inc(sem("weights_in"), 16)
            with sp.Fori(0, CT) as i:
                for half in range(2):
                    sp.wait_ge(sem(f"normed{half}_3"), i + 2)
                    sp.dma_start(outs[half][bass.ds(i, 1)].rearrange("o p n -> (o p) n"),
                                 normed[half][:].rearrange("p q n -> p (q n)")).then_inc(sem(f"out{half}"), 16)
            for half in range(2):
                sp.wait_ge(sem(f"out{half}"), 16 * (CT + 1))
            sp.wait_ge(sem("weights_in"), 16 * 3)

        @block.tensor
        def _(pe):
            def project(i, half, q):
                pe.wait_ge(sem(f"squared{1 - half}_{q}"), i + 1 + half)
                pe.wait_ge(sem(f"copied{1 - half}_{q}"), i + 1 + half)
                for k in range(KT):
                    last = pe.matmul(banks[:, q], w[half][:, k, :], c.h_t[:, k, q * N512:(q + 1) * N512],
                                     start=k == 0, stop=k == KT - 1)
                last.then_inc(sem(f"product{half}_{q}"), 1)

            def sum_squares(i, half, q):
                pe.wait_ge(sem(f"squared{half}_{q}"), i + 2)
                before = f"logged{half}_{q - 2}" if q >= 2 else f"logged{1 - half}_{q + 2}"
                pe.wait_ge(sem(before), i + (2 if q >= 2 else 1 + half))
                pe.matmul(banks[0:2, 4 + q % 2], c.all_heads[:, 0, 0:2], square[:, q, :], start=True, stop=True).then_inc(
                    sem(f"summed{half}_{q}"), 1)

            def widen(i, half, q):
                before = f"normed{half}_{q - 2}" if q >= 2 else f"normed{1 - half}_{q + 2}"
                pe.wait_ge(sem(before), i + (2 if q >= 2 else 1 + half))
                pe.wait_ge(sem(f"rstd{half}_{q}"), i + 2)
                pe.matmul(banks[:, 6 + q % 2], c.head_rows[0:2, 0:P], rstd[:, q, :], start=True,
                          stop=True).then_inc(sem(f"widened{half}_{q}"), 1)

            with pe.Fori(0, CT) as i:
                for half in range(2):
                    pe.wait_ge(sem(f"w_in{half}"), 16 * i + 16)
                    for q in range(6):
                        if q < 4:
                            project(i, half, q)
                        if 1 <= q < 5:
                            sum_squares(i, half, q - 1)
                        if q >= 2:
                            widen(i, half, q - 2)

        @block.scalar
        def _(act):
            act.preload_act_table_set("natural_log_exp_and_others")

            def inverse_root(i, half, q):
                act.wait_ge(sem(f"rstd{1 - half}_{q}"), i + 1 + half)
                act.wait_ge(sem(f"summed{half}_{q}"), i + 2)
                act.activation(logged[:, q, :], banks[0:2, 4 + q % 2], ACT.Ln, scale=1.0 / HD,
                               bias=c.eps[0:2, 0:1]).then_inc(sem(f"logged{half}_{q}"), 1)
                act.wait_ge(sem(f"widened{1 - half}_{q}"), i + 1 + half)
                act.wait_ge(sem(f"logged{half}_{q}"), i + 2)
                act.activation(rstd[:, q, :], logged[:, q, :], ACT.Exp, scale=-0.5).then_inc(
                    sem(f"rstd{half}_{q}"), 1)

            for half in range(2):
                first = RW_IN + half * RW
                act.dma_start(w[half][:], w_tiles[:, :, first:first + P]).then_inc(sem(f"w_in{half}"), 16)
            with act.Fori(0, CT) as i:
                for half in range(2):
                    for q in range(4):
                        act.wait_ge(sem(f"normed{1 - half}_{q}"), i + 1 + half)
                        act.wait_ge(sem(f"product{half}_{q}"), i + 2)
                        act.copy(u[:, q, :], banks[:, q]).then_inc(sem(f"copied{half}_{q}"), 1)
                        act.wait_ge(sem(f"summed{1 - half}_{q}"), i + 1 + half)
                        act.activation(square[:, q, :], banks[:, q], ACT.Square).then_inc(
                            sem(f"squared{half}_{q}"), 1)
                        if q >= 1:
                            inverse_root(i, half, q - 1)
                    inverse_root(i, half, 3)
                    act.dma_start(w[half][:], w_tiles[:, :, bass.ds((i + 1) * P + (RW_IN + half * RW), P)]).then_inc(
                        sem(f"w_in{half}"), 16)
            for half in range(2):
                act.wait_ge(sem(f"w_in{half}"), 16 * (CT + 1))

        def norm(dve, i, half, q):
            dve.wait_ge(sem(f"copied{half}_{q}"), i + 2)
            dve.wait_ge(sem(f"widened{half}_{q}"), i + 2)
            dve.scalar_tensor_tensor(out=normed[half][:, q, :], in0=u[:, q, :], scalar=gain[:, half:half + 1],
                                     in1=banks[:, 6 + q % 2], op0=ALU.mult, op1=ALU.mult).then_inc(
                sem(f"normed{half}_{q}"), 1)

        @block.vector
        def _(dve):
            dve.wait_ge(sem("gain_in"), 16 * 4)
            dve.tensor_scalar(gain[:, 0:1], gain[:, 0:1], HD ** -0.5, None, ALU.mult).then_inc(sem("gain_scaled"), 1)
            dve.wait_ge(sem("gain_scaled"), 1)
            with dve.Fori(0, CT) as i:
                for half in range(2):
                    dve.wait_ge(sem(f"out{half}"), 16 * i + 16)
                    for q in range(4):
                        norm(dve, i, half, q)


def load_mixer(nc, a, c, m, dram, banks):
    with ExitStack() as stack:
        sb = Memory(nc, stack, "load")
        sem = Signals(nc, stack, "load")
        mem = sb("mem", P, MT, DM)
        squares = sb("squares", P, MT, DM)
        square_sum = sb("square_sum", P, MT)
        logged = sb("logged", P, MT)
        rstd = sb("rstd", P, MT)
        mem_t = sb("mem_t", P, KT, N_MEM)
        w_kv = sb("w_kv", P, KT, 2 * XW)
        gain_mem = sb("gain_mem", P, KT)
        gain_k = sb("gain_k", P, 1)
        k_rows = sb("k_rows", P, MT, XW)
        k_squares = sb("k_squares", P, MT, XW)
        k_sum = sb("k_sum", P, MT * XH)
        k_logged = sb("k_logged", P, MT * XH)
        k_rstd = sb("k_rstd", P, MT * XH)
        raw_k_a = sb("raw_k_a", P, CT)
        block = stack.enter_context(nc.Block())

        @block.sync
        def _(sp):
            sp.dma_start(mem[:], a["mem"][0].rearrange("(t p) d -> p t d", p=P)).then_inc(sem("mem_in"), 16)
            sp.dma_start(w_kv[:], a["xa_w_kv"][0].rearrange("(k p) n -> p k n", p=P)).then_inc(sem("w_kv_in"), 16)
            with nc.allow_non_contiguous_dma(reason="gain vectors over partitions"):
                for tile, name, tiles in ((gain_mem, "norm_mem", KT), (gain_k, "xa_k_norm", 1),
                                          (raw_k_a, "rw_k_a", CT), (m.w0, "decay_w0", CT), (m.a0, "iclr_a0", CT),
                                          (m.gain_kk, "rw_k_k", CT), (m.ln_w, "lnx_w", CT), (m.ln_b, "lnx_b", CT),
                                          (m.gain_att, "att_out_norm", CT), (m.gain_xa, "norm_xa", KT), (m.gain_ffn, "norm_ffn", KT),
                                          (m.gain_q, "xa_q_norm", 1)):
                    sp.dma_start(tile[:], column(a[name][0], tiles)).then_inc(sem("gains_in"), 16)
                sp.dma_start(m.r_k[:], column(a["rw_r_k"][0].rearrange("h n -> (h n)"), CT)).then_inc(
                    sem("gains_in"), 16)
                sp.dma_start(m.w_router[:, :, 0:GROUPS], a["moe_w_group"][0].rearrange("(k p) n -> p k n", p=P)
                             ).then_inc(sem("weights_in"), 16)
                sp.dma_start(m.w_router[:, :, GROUPS:LOGITS], a["moe_w_route"][0].rearrange(
                    "(k p) n -> p k n", p=P)).then_inc(sem("weights_in"), 16)
            sp.dma_start(m.b_router[:, 0:GROUPS], a["moe_b_group"].broadcast_to([P, GROUPS])).then_inc(
                sem("weights_in"), 16)
            sp.dma_start(m.b_router[:, GROUPS:LOGITS], a["moe_b_route"].broadcast_to([P, EXPERTS])).then_inc(
                sem("weights_in"), 16)
            sp.dma_start(m.lora_wa[0:LORA, :], a["decay_w2"][0]).then_inc(sem("weights_in"), 16)
            sp.dma_start(m.lora_wa[LORA:P, :], a["iclr_a2"][0]).then_inc(sem("weights_in"), 16)
            sp.dma_start(m.gate[:], a["gate_g2"][0]).then_inc(sem("weights_in"), 16)
            sp.wait_ge(sem("weights_in"), 16 * 7)

        @block.gpsimd
        def _(pool):
            pool.dma_start(m.bias[:], a["att_rel_bias"]).then_inc(sem("bias_in"), 16)
            pool.wait_ge(sem("bias_in"), 16)
            pool.memset(m.bias[0:CHUNK, :, BAND - CHUNK:BAND], NEG).then_inc(sem("bias_masked"), 1)
            pool.memset(m.bias[CHUNK:P, :, 0:CHUNK], NEG).then_inc(sem("bias_masked"), 1)
            pool.wait_ge(sem("bias_masked"), 2)
            pool.dma_start(dram["bias"], m.bias[:]).then_inc(sem("bias_out"), 16)
            pool.wait_ge(sem("bias_out"), 16)
            pool.memset(m.bias[:, :, 0:PREV], NEG).then_inc(sem("past_masked"), 1)
            pool.memset(m.state[:], 0.0).then_inc(sem("past_masked"), 1)
            pool.memset(m.shift_back[:], 10 * float(np.log(2.0))).then_inc(sem("past_masked"), 1)
            pool.wait_ge(sem("past_masked"), 3)

        @block.scalar
        def _(act):
            act.preload_act_table_set("natural_log_exp_and_others")
            act.wait_ge(sem("mem_in"), 16)
            for t in range(MT):
                act.activation(squares[:, t, :], mem[:, t, :], ACT.Square, accum_out=square_sum[:, t:t + 1]).then_inc(
                    sem("squared"), 1)
            act.wait_ge(sem("squared"), MT)
            act.activation(logged[:], square_sum[:], ACT.Ln, scale=1.0 / DM, bias=c.eps[:, 0:1]).then_inc(
                sem("logged"), 1)
            act.wait_ge(sem("logged"), 1)
            act.activation(rstd[:], logged[:], ACT.Exp, scale=-0.5).then_inc(sem("rstd"), 1)
            for t in range(MT):
                act.wait_ge(sem("kv"), 2 * t + 2)
                act.copy(m.v_mem[:, t, :], banks[:, 2 * t + 1]).then_inc(sem("v_kept"), 1)
                act.activation(k_squares[:, t, :], banks[:, 2 * t], ACT.Square).then_inc(sem("k_squared"), 1)
            act.wait_ge(sem("k_summed"), 1)
            act.activation(k_logged[:], k_sum[:], ACT.Ln, scale=1.0 / XD, bias=c.eps[:, 0:1]).then_inc(
                sem("k_logged"), 1)
            act.wait_ge(sem("k_logged"), 1)
            act.activation(k_rstd[:], k_logged[:], ACT.Exp, scale=-0.5).then_inc(sem("k_rstd"), 1)
            act.wait_ge(sem("v_kept"), MT)

        @block.vector
        def _(dve):
            dve.wait_ge(sem("rstd"), 1)
            for t in range(MT):
                dve.tensor_scalar(mem[:, t, :], mem[:, t, :], rstd[:, t:t + 1], None, ALU.mult).then_inc(
                    sem("mem_scaled"), 1)
            dve.wait_ge(sem("gains_in"), 16 * 13)
            for t in range(MT):
                dve.wait_ge(sem("mem_turned"), t + 1)
                dve.tensor_tensor(mem_t[:, :, t * P:(t + 1) * P],
                                  banks[:, 2 * t:2 * t + 2].rearrange("p b (k t) -> p (b k) t", t=P),
                                  spread(gain_mem[:], P), ALU.mult).then_inc(sem("mem_t"), 1)
            dve.tensor_scalar(m.half_k_a[:], raw_k_a[:], 0.5, None, ALU.mult).then_inc(sem("half_k_a"), 1)
            dve.tensor_scalar(m.rest_k_a[:], raw_k_a[:], -0.5, 1.0, ALU.mult, ALU.add).then_inc(sem("half_k_a"), 1)
            dve.tensor_scalar(m.scaled_q[:], m.gain_q[:], XD ** -0.5, None, ALU.mult).then_inc(sem("half_k_a"), 1)
            dve.wait_ge(sem("k_squared"), MT)
            dve.tensor_reduce(k_sum[:], k_squares[:].rearrange("p t (h d) -> p (t h) d", d=XD), AX.X,
                              ALU.add).then_inc(sem("k_summed"), 1)
            dve.wait_ge(sem("k_rstd"), 1)
            for t in range(MT):
                dve.tensor_tensor(k_rows[:, t, :].rearrange("p (h d) -> p h d", d=XD),
                                  banks[:, 2 * t].rearrange("p (h d) -> p h d", d=XD),
                                  spread(k_rstd[:, t * XH:(t + 1) * XH], XD), ALU.mult).then_inc(
                    sem("k_normed"), 1)
            for t in range(MT):
                dve.wait_ge(sem("k_turned"), t + 1)
                dve.tensor_scalar(m.k_mem[:, :, t * P:(t + 1) * P], banks[:, 4 + t].rearrange(
                    "p (h t) -> p h t", t=P), gain_k[:, 0:1], None, ALU.mult).then_inc(sem("k_kept"), 1)
            dve.wait_ge(sem("k_kept"), MT)
            dve.wait_ge(sem("half_k_a"), 3)

        @block.tensor
        def _(pe):
            for t in range(MT):
                pe.wait_ge(sem("mem_scaled"), t + 1)
                for k in range(KT):
                    last = pe.transpose(banks[:, 2 * t + k // 4, (k % 4) * P:(k % 4 + 1) * P],
                                        mem[:, t, k * P:(k + 1) * P], c.ident[:])
                last.then_inc(sem("mem_turned"), 1)
            pe.wait_ge(sem("mem_t"), MT)
            pe.wait_ge(sem("w_kv_in"), 16)
            for t in range(MT):
                for n in range(2):
                    for k in range(KT):
                        last = pe.matmul(banks[:, 2 * t + n], mem_t[:, k, t * P:(t + 1) * P],
                                         w_kv[:, k, n * XW:(n + 1) * XW], start=k == 0, stop=k == KT - 1)
                    last.then_inc(sem("kv"), 1)
            for t in range(MT):
                pe.wait_ge(sem("k_normed"), t + 1)
                for h in range(XH):
                    last = pe.transpose(banks[:, 4 + t, h * P:(h + 1) * P], k_rows[:, t, h * XD:(h + 1) * XD],
                                        c.ident[:])
                last.then_inc(sem("k_turned"), 1)


STEPS = """
    lora head0 decay head1 head2 head3 key_sum key_norm head4 weigh turn0 head5 turn1 pairs first_level head6
    cross1 head7 grow1 head8 head9 att_rec cross2 att_wide grow2 att_norm join0 cross3 join1 join2 grow3 join3
    cross4 xa_norm grow4 xa_rows cross5 xa_query grow5 target0 xa_turn solve0 xa_score output0 xa_exp target1
    xa_weigh xa_read solve1 xa_out output1 ffn_norm center ffn_turn variance gate route att_gain
""".split()
TAIL_STEPS = """
    join0 join1 join2 join3 xa_norm xa_rows xa_query xa_turn xa_score xa_exp xa_weigh xa_read xa_out ffn_norm
    ffn_turn route
""".split()


def mix_tokens(nc, a, c, m, dram, banks):
    with ExitStack() as stack:
        sb = Memory(nc, stack, "mix")
        turns = """tanh_w tanh_g gate_in lora_w lora_a lora_g z_w z_a tanh_zw tanh_za log_decay decay_sum
            decay_before decayed grown decayed_before kk_raw kk_squared kk_sum kk_floor kk_logged kk_rstd kk_wide kk
            a_now kk_a a_tilde b_tilde k_weight k_new k_tilde r_tilde r_k_raw r_k_pair
            p3_done p1_done0 p1_done1 p2_done0 p2_done1 p3_masked inverse inverse_t p1_kept0 p1_kept1 first_t
            p2_kept0 p2_kept1 y_kept y_mean y_center y_square y_var y_logged y_rstd y_wide y_norm y_affine bonus_done
            bonus_v y_bonus y_out joined x2 x2_squared x2_logged x2_rstd x2_scaled x2_turned hx xq xq_squared
            xq_summed xq_logged xq_rstd xq_normed xq_turned xq_t xs_done xs_max xs_negmax xp xp_rstd xp_normed
            xp_turned xp_t xo_done xo_t xout x3 x3_squared x3_logged x3_rstd h_ffn h_ffn_turned h_ffn_t logits_done
            logits att_rec rec_turned rec_t rec_wide att_raw att_y att_squared att_summed att_logged att_rstd
            att_scaled att_t""".split()
        turns += [f"turned_{n}" for n in "vbk"] + [f"{n}_rows{p}" for n in "vbk" for p in range(2)]
        turns += [f"{s}{p}" for s in ("target", "target_kept", "solved", "u", "y_done", "state_sum", "state_added",
                                      "state") for p in range(2)]
        turns += ["cross_done", "cross_kept", "grow_done", "grow_t_done", "inverse_new", "inverse_t_new"]
        turns += ["scores", "score_neg", "prob", "prob_turned", "prob_t", "read"]
        dmas = "rk_in v_in wag_in x_in x3_out h_out bias_in".split()
        sem = Signals(nc, stack, "mix", " ".join(turns), " ".join(dmas))
        nc.gpsimd.sem_inc(sem("begun"), 1)

        def need(engine, t, *names):
            for name in names:
                engine.wait_ge(sem(name), t * 16 + 32 if name in dmas else t + 2)

        def after(t):
            return t if isinstance(t, int) else t + 1

        def tail_before(engine, t, *names):
            if not isinstance(t, int):
                for name in names:
                    engine.wait_ge(sem(name), t)

        def freed(engine, t, *names):
            for name in names:
                engine.wait_ge(sem(name), t * 16 + 16 if name in dmas else t + 1)

        def apart(engine):
            engine.wait_ge(sem("begun"), 1)

        registers = {}

        def worked_out(engine, value):
            if isinstance(value, int):
                return value
            if engine not in registers:
                registers[engine] = engine.alloc_register(f"value{len(registers)}")
            engine.reg_mov(registers[engine], value)
            return registers[engine]

        def need_nth(engine, t, name, n, per, alone=False):
            count = t * per + (n + 2)
            if isinstance(t, int):
                if count > 0:
                    engine.wait_ge(sem(name), count)
            else:
                if alone:
                    count = worked_out(engine, count)
                    apart(engine)
                engine.wait_ge(sem(name), count)

        def need_band(engine, t, j):
            engine.wait_ge(sem(f"band_in{j % 2}"), t * 96 + (j // 2 + 1) * 48)

        LV = len(LEVELS) - 1
        f4 = [P, CT, P]
        rk, v_now, wag = sb("rk", P, 2, CT, P), sb("v", *f4), sb("wag", P, 2, P)
        lora_in, gate_half, gate_in = sb("lora_in", LORA, P), sb("gate_half", P, P), sb("gate_in", P, P)
        decay_path, sum_path, iclr_path = sb("decay_path", *f4), sb("sum_path", *f4), sb("iclr_path", *f4)
        decayed = sb("decayed", *f4)
        kk, kk_a, rw_squares = sb("kk", *f4), sb("kk_a", *f4), sb("rw_squares", *f4)
        head_sum, head_rstd = sb("head_sum", HEADS, P), sb("head_rstd", HEADS, P)
        a_and_r = sb("a_and_r", P, CT, 2, 2, CHUNK)
        b_tilde, k_tilde = sb("b_tilde", *f4), sb("k_tilde", *f4)
        v_rows, b_rows, k_rows = (sb(n, P, 2, CT, HD) for n in ("v_rows", "b_rows", "k_rows"))
        PAIRS = 2 * CT
        from_b, from_k = sb("from_b", P, PAIRS, P), sb("from_k", P, PAIRS, P)
        inverse, inverse_t, cross = (sb(n, P, PAIRS, HD) for n in ("inverse", "inverse_t", "cross"))
        target, u, state_sum = (sb(n, P, CT, HD) for n in ("target", "u", "state_sum"))
        y, y_center, y_out = (sb(n, *f4) for n in ("y", "y_center", "y_out"))
        q_pair, k_pair, v_pair = ([sb(f"{n}{i}", *shape) for i in range(2)] for n, shape in (
            ("q_pair", [P, P]), ("k_pair", [P, BAND]), ("v_pair", [P, KB, P])))
        scores_2 = sb("scores_2", P, 2 * BAND)
        score = [scores_2[:, i * BAND:(i + 1) * BAND] for i in range(2)]
        xp = scores_2[:, 0:XH * N_MEM].rearrange("p (h n) -> p h n", n=N_MEM)
        turned_2 = sb("turned_2", P, 2 * BAND)
        prob_t = [turned_2[:, i * BAND:(i + 1) * BAND] for i in range(2)]
        xp_t = turned_2[:, 0:XH * N_MEM].rearrange("p (h n) -> p h n", n=P)
        neg_max, row_sum, row_rec = (sb(n, P, HEADS) for n in ("neg_max", "row_sum", "row_rec"))
        att_y, att_t = sb("att_y", *f4), sb("att_t", *f4)
        xq_normed, xqo_t = turned_2[:, 0:XW], att_t
        att_squares = scores_2[:, 0:RW]
        att_rstd, rec_t = scores_2[:, RW:RW + P], scores_2[0:HEADS, RW + P:RW + 2 * P]
        x_now, normed = sb("x", P, DM), sb("normed", P, DM)
        x2_sum, x2_logged, x2_rstd, x3_sum, x3_logged, x3_rstd = (sb(n, P, 1) for n in (
            "x2_sum", "x2_logged", "x2_rstd", "x3_sum", "x3_logged", "x3_rstd"))
        normed_t = sb("normed_t", P, KT, P)
        xq_sum, xq_logged, xq_rstd, xs_max, xs_negmax, xp_sum, xp_rec = (sb(n, P, XH) for n in (
            "xq_sum", "xq_logged", "xq_rstd", "xs_max", "xs_negmax", "xp_sum", "xp_rec"))

        R0, R1, R2 = banks[:, 0], banks[:, 1], banks[:, 2]
        S = banks[:, 3:5].rearrange("p b n -> p (b n)")
        T = banks[:, 5:7].rearrange("p b n -> p (b n)")
        V = banks[:, 7]

        def tiles(bank, n=P):
            return bank.rearrange("p (c n) -> p c n", n=n)

        def by_chunk(ap):
            return ap[:].rearrange("p c (q n) -> p c q n", n=CHUNK)

        HALVES = (slice(0, HD), slice(HD, P))
        first_steps = [s for s in STEPS if s not in TAIL_STEPS]
        block = stack.enter_context(nc.Block())

        def run(engine, steps):
            for s in first_steps:
                if s in steps:
                    steps[s](0)
            with engine.Fori(1, TILES) as t:
                for s in STEPS:
                    if s in steps:
                        steps[s](t - 1 if s in TAIL_STEPS else t)
            for s in TAIL_STEPS:
                if s in steps:
                    steps[s](TILES - 1)

        @block.sync
        def _(sp):
            def load(t, out, in_, name, *frees):
                apart(sp)
                freed(sp, t, *frees)
                sp.dma_start(out, in_).then_inc(sem(name), 16)

            def bands(t, which):
                now = bass.ds(t * P, P)
                for j in which:
                    need_nth(sp, t, "read", 2 * j - 3, HEADS)
                    band = sem(f"band_in{j % 2}")
                    sp.dma_start(q_pair[j % 2][:], dram["q"][j, :, now]).then_inc(band, 16)
                    sp.dma_start(k_pair[j % 2][:], dram["k"][j, :, bass.ds(t * P, BAND)]).then_inc(band, 16)
                    sp.dma_start(v_pair[j % 2][:], dram["v"][bass.ds(t * P, BAND), j * P:(j + 1) * P].rearrange(
                        "(b p) d -> p b d", p=P)).then_inc(band, 16)

            def front(t):
                now = bass.ds(t * P, P)
                bands(t, (0, 1))
                load(t, wag[:], dram["rw"][12:14, :, now].rearrange("c p n -> p c n"), "wag_in", "tanh_w", "tanh_g",
                     "lora_a")
                load(t, rk[:], dram["rw"][0:8, :, now].rearrange("(s c) p n -> p s c n", s=2), "rk_in", "kk_raw",
                     "k_new", "r_tilde", "r_k_raw")
                load(t, v_now[:], dram["rw"][8:12, :, now].rearrange("c p n -> p c n"), "v_in", "turned_v", "bonus_v")
                bands(t, (2, 3))

            def past(t):
                need_nth(sp, t, "score_neg", HEADS - 1, HEADS, alone=True)
                block_at = bass.ds((TILES + 3 - t) % 4 * P, P)
                sp.dma_start(m.bias[:, :, block_at], dram["bias"][:, :, block_at]).then_inc(sem("bias_in"), 16)

            def residual(t):
                load(t, x_now[:], a["x"][0, bass.ds(t * P, P), :], "x_in", "x3_out", "h_ffn",
                     "x3_squared")

            front(0)
            past(0)
            with sp.Fori(1, TILES) as t:
                front(t)
                residual(t - 1)
                past(t)
            residual(TILES - 1)
            for name in ("bias_in", "x3_out", "h_out"):
                sp.wait_ge(sem(name), 16 * (TILES + 1))

        @block.tensor
        def _(pe):
            def lora(t):
                freed(pe, t, "bonus_v")
                need(pe, t, "tanh_w")
                for k in range(CT):
                    last = pe.matmul(R0[:, k * P:(k + 1) * P], m.lora_wa[0:LORA, k * P:(k + 1) * P], lora_in[:],
                                     start=True, stop=True)
                last.then_inc(sem("lora_w"), 1)
                freed(pe, t, "y_norm")
                need(pe, t, "wag_in")
                for k in range(CT):
                    last = pe.matmul(R1[:, k * P:(k + 1) * P], m.lora_wa[LORA:P, k * P:(k + 1) * P], wag[LORA:P, 0, :],
                                     start=True, stop=True)
                last.then_inc(sem("lora_a"), 1)

            def sum_heads(bank, squares_of):
                for k in range(CT):
                    last = pe.matmul(bank[0:HEADS, 0:P], c.all_heads[:, k, :], squares_of[:, k, :], start=k == 0,
                                     stop=k == CT - 1)
                return last

            def widen(bank, heads):
                for k in range(CT):
                    last = pe.matmul(bank[:, k * P:(k + 1) * P], c.head_rows[:, k * P:(k + 1) * P], heads,
                                     start=True, stop=True)
                return last

            def key_sum(t):
                need(pe, t, "z_w", "kk_squared")
                sum_heads(R0, rw_squares).then_inc(sem("kk_sum"), 1)

            def key_norm(t):
                need(pe, t, "z_a", "kk_rstd")
                widen(R1, head_rstd[:]).then_inc(sem("kk_wide"), 1)

            def turn_rows(bank, source, name):
                for k in range(CT):
                    last = pe.transpose(bank[:, k * P:(k + 1) * P], source[:, k, :], c.ident[:])
                last.then_inc(sem(name), 1)

            def turn0(t):
                need(pe, t, "v_in")
                freed(pe, t, "y_out")
                turn_rows(R2, v_now, "turned_v")
                need(pe, t, "kk", "b_tilde")
                turn_rows(R1, b_tilde, "turned_b")

            def turn1(t):
                need(pe, t, "kk_floor", "k_tilde")
                turn_rows(R0, k_tilde, "turned_k")

            def pairs(t):
                def with_a_and_r(bank, left, p):
                    for k in range(CT):
                        for rows in HALVES:
                            chunk = slice(p * CHUNK, (p + 1) * CHUNK)
                            last = pe.matmul(bank[rows, k * P:(k + 1) * P], left[rows, k, chunk],
                                             a_and_r[rows, k, p].rearrange("p s n -> p (s n)"), start=True, stop=True)
                    return last

                apart(pe)
                need(pe, t, "v_rows0", "v_rows1", "a_tilde")
                for p in range(2):
                    chunk = slice(p * CHUNK, (p + 1) * CHUNK)
                    for k in range(CT):
                        for rows in HALVES:
                            n = (p * CT + k) * HD
                            last = pe.matmul(R2[rows, n:n + HD], a_and_r[rows, k, p, 0], b_tilde[rows, k, chunk],
                                             start=True, stop=True)
                last.then_inc(sem("p3_done"), 1)
                apart(pe)
                need(pe, t, "k_rows0", "k_rows1", "r_tilde")
                with_a_and_r(R0, b_tilde, 0).then_inc(sem("p1_done0"), 1)
                apart(pe)
                need(pe, t, "b_rows0", "b_rows1")
                with_a_and_r(R1, b_tilde, 1).then_inc(sem("p1_done1"), 1)
                apart(pe)
                need(pe, t, "p3_masked")
                with_a_and_r(R2, k_tilde, 0).then_inc(sem("p2_done0"), 1)
                apart(pe)
                need(pe, t, "p1_kept0")
                with_a_and_r(R0, k_tilde, 1).then_inc(sem("p2_done1"), 1)

            def all_pairs(bank, left, right):
                for n in range(PAIRS):
                    for rows in HALVES:
                        last = pe.matmul(bank[rows, n * HD:(n + 1) * HD], left[rows, n, 0:HD], right[rows, n, :],
                                         start=True, stop=True)
                return last

            def cross_products(n):
                def step(t):
                    apart(pe)
                    if n == 1:
                        need(pe, t, "p1_kept1", "inverse")
                    else:
                        need_nth(pe, t, "inverse_new", n - 2, LV - 1, alone=True)
                        need_nth(pe, t, "cross_kept", n - 2, LV, alone=True)
                    all_pairs(R1, from_b, inverse).then_inc(sem("cross_done"), 1)
                return step

            def grow(n):
                def step(t):
                    apart(pe)
                    if n == 1:
                        need(pe, t, "p2_kept0", "p2_kept1", "inverse_t")
                    else:
                        need_nth(pe, t, "inverse_t_new", n - 2, LV)
                    need_nth(pe, t, "cross_kept", n - 1, LV, alone=True)
                    if n < LV:
                        all_pairs(R2, inverse_t, cross).then_inc(sem("grow_done"), 1)
                    all_pairs(R0, cross, inverse_t).then_inc(sem("grow_t_done"), 1)
                return step

            def solve_target(p):
                def step(t):
                    bank = (R1, R2)[p]
                    apart(pe)
                    if p == 0:
                        need_nth(pe, t, "cross_kept", LV - 1, LV)
                        freed(pe, t, "state1")
                    else:
                        need(pe, t, "u0", "state0")
                    for k in range(CT):
                        for rows in HALVES:
                            out = bank[rows, k * HD:(k + 1) * HD]
                            pe.matmul(out, a_and_r[rows, k, p, 0], m.state[rows, k, :], start=True, stop=False)
                            last = pe.matmul(out, from_k[rows, p * CT + k, 0:HD], v_rows[rows, p, k, :],
                                             start=False, stop=True)
                    last.then_inc(sem(f"target{p}"), 1)
                return step

            def solve(p):
                def step(t):
                    bank = (R2, R1)[p]
                    apart(pe)
                    need(pe, t, f"target_kept{p}")
                    if p == 0:
                        need_nth(pe, t, "inverse_t_new", LV - 1, LV)
                        need_nth(pe, t, "inverse_new", LV - 2, LV - 1)
                    else:
                        need(pe, t, "state_added0")
                    for k in range(CT):
                        for rows in HALVES:
                            last = pe.matmul(bank[rows, k * HD:(k + 1) * HD], inverse_t[rows, p * CT + k, :],
                                             target[rows, k, :], start=True, stop=True)
                    last.then_inc(sem(f"solved{p}"), 1)
                return step

            def output(p):
                def step(t):
                    bank = (R1, R2)[p]
                    chunk = slice(p * CHUNK, (p + 1) * CHUNK)
                    apart(pe)
                    need(pe, t, f"u{p}")
                    for k in range(CT):
                        for rows in HALVES:
                            out = R0[rows, k * P + p * CHUNK:k * P + (p + 1) * CHUNK]
                            n = p * CT + k
                            pe.matmul(out, m.state[rows, k, :], a_and_r[rows, k, p, 1], start=True, stop=False)
                            pe.matmul(out, u[rows, k, :], from_b[rows, n, HD:P], start=False, stop=False)
                            last = pe.matmul(out, v_rows[rows, p, k, :], from_k[rows, n, HD:P], start=False,
                                             stop=True)
                    last.then_inc(sem(f"y_done{p}"), 1)
                    for k in range(CT):
                        for rows in HALVES:
                            out = bank[rows, k * HD:(k + 1) * HD]
                            pe.matmul(out, b_rows[rows, p, k, :], u[rows, k, :], start=True, stop=False)
                            last = pe.matmul(out, k_rows[rows, p, k, :], v_rows[rows, p, k, :], start=False,
                                             stop=True)
                    last.then_inc(sem(f"state_sum{p}"), 1)
                return step

            def center(t):
                need(pe, t, "y_kept", "u1")
                pe.matmul(R1, c.same_head[:], y[:].rearrange("p c n -> p (c n)"), start=True, stop=True).then_inc(
                    sem("y_mean"), 1)

            def variance(t):
                need(pe, t, "r_k_pair")
                pe.matmul(R0, c.same_head[:], iclr_path[:].rearrange("p c n -> p (c n)"), start=True,
                          stop=True).then_inc(sem("bonus_done"), 1)
                need(pe, t, "y_square", "state_added1")
                sum_heads(R2, rw_squares).then_inc(sem("y_var"), 1)

            def gate_y(t):
                need(pe, t, "y_rstd")
                widen(R1, head_rstd[:]).then_inc(sem("y_wide"), 1)
                need(pe, t, "y_logged", "gate_in")
                for k in range(CT):
                    last = pe.matmul(R2[:, k * P:(k + 1) * P], m.gate[:, k * P:(k + 1) * P], gate_in[:], start=True,
                                     stop=True)
                last.then_inc(sem("lora_g"), 1)

            def join(n):
                def step(t):
                    if n == 0:
                        need(pe, t, "y_out", "att_t")
                        need_nth(pe, after(t), "score_neg", HEADS - 1, HEADS)
                    columns = slice(n // 2 * N512, (n // 2 + 1) * N512)
                    for k in range(CT):
                        left = (y_out, att_t)[n % 2]
                        last = pe.matmul(S[:, columns], left[:, k, :], m.w_out[:, (n % 2) * CT + k, columns],
                                         start=n % 2 == 0 and k == 0, stop=n % 2 == 1 and k == CT - 1)
                    if n == 3:
                        last.then_inc(sem("joined"), 1)
                return step

            def turn_row(source, count, name):
                for k in range(count):
                    last = pe.transpose(T[:, k * P:(k + 1) * P], source[:, k * P:(k + 1) * P], c.ident[:])
                last.then_inc(sem(name), 1)

            def xa_rows(t):
                need(pe, t, "x2_scaled")
                need(pe, after(t), "att_logged")
                turn_row(normed, KT, "x2_turned")

            def xa_query(t):
                need(pe, t, "hx")
                need(pe, after(t), "att_raw")
                for k in range(KT):
                    last = pe.matmul(V, normed_t[:, k, :], m.w_q[:, k, :], start=k == 0, stop=k == KT - 1)
                last.then_inc(sem("xq"), 1)

            def xa_turn(t):
                need(pe, t, "xq_normed")
                turn_row(xq_normed, XH, "xq_turned")

            def xa_score(t):
                need(pe, t, "xq_t", "x2")
                for h in range(XH):
                    last = pe.matmul(S[:, h * N_MEM:(h + 1) * N_MEM], xqo_t[:, h, :], m.k_mem[:, h, :], start=True,
                                     stop=True)
                last.then_inc(sem("xs_done"), 1)

            def xa_weigh(t):
                need(pe, t, "xp_normed")
                turn_row(scores_2, XH * MT, "xp_turned")

            def xa_read(t):
                need(pe, t, "xp_t")
                for h in range(XH):
                    for j in range(MT):
                        last = pe.matmul(V[:, h * P:(h + 1) * P], m.v_mem[:, j, h * XD:(h + 1) * XD],
                                         xp_t[:, h * MT + j, :], start=j == 0, stop=j == MT - 1)
                last.then_inc(sem("xo_done"), 1)

            def xa_out(t):
                need(pe, t, "xo_t", "xp")
                for n in range(2):
                    for h in range(XH):
                        last = pe.matmul(S[:, n * N512:(n + 1) * N512], xqo_t[:, h, :],
                                         m.w_o[:, h, n * N512:(n + 1) * N512], start=h == 0, stop=h == XH - 1)
                last.then_inc(sem("xout"), 1)

            def ffn_turn(t):
                need(pe, t, "h_ffn")
                turn_row(normed, KT, "h_ffn_turned")

            def route(t):
                need(pe, t, "h_ffn_t")
                for k in range(KT):
                    last = pe.matmul(V[:, 0:LOGITS], normed_t[:, k, :], m.w_router[:, k, :], start=k == 0,
                                     stop=k == KT - 1)
                last.then_inc(sem("logits_done"), 1)

            def head(h):
                def step(t):
                    if h < HEADS:
                        if h == 0:
                            tail_before(pe, t, "x3")
                        if h % 2 == 0:
                            need_band(pe, t, h // 2)
                        need_nth(pe, t, "score_neg", h - 1, HEADS)
                        rows, j = HALVES[h % 2], h // 2 % 2
                        pe.matmul(S[:, 0:N512], q_pair[j][rows, :], k_pair[j][rows, 0:N512], start=True, stop=True)
                        pe.matmul(S[:, N512:BAND], q_pair[j][rows, :], k_pair[j][rows, N512:BAND], start=True,
                                  stop=True).then_inc(sem("scores"), 1)
                    if 1 <= h <= HEADS:
                        if h == 1:
                            tail_before(pe, t, "h_ffn_t")
                        need_nth(pe, t, "prob_t", h - 2, HEADS)
                        need_nth(pe, t, "prob", h - 1, HEADS)
                        for j in range(KB):
                            last = pe.transpose(T[:, j * P:(j + 1) * P], score[(h - 1) % 2][:, j * P:(j + 1) * P],
                                                c.ident[:])
                        last.then_inc(sem("prob_turned"), 1)
                    if h >= 2:
                        if h == 2:
                            tail_before(pe, t, "logits")
                        need_nth(pe, t, "prob_t", h - 2, HEADS)
                        columns = slice((h - 2) // 2 * P, h // 2 * P)
                        for j in range(KB):
                            last = pe.matmul(V[HALVES[h % 2], columns], v_pair[(h - 2) // 2 % 2][:, j, HALVES[h % 2]],
                                             prob_t[h % 2][:, j * P:(j + 1) * P], start=j == 0, stop=j == KB - 1)
                        last.then_inc(sem("read"), 1)
                return step

            def att_rec(t):
                need(pe, t, "att_rec")
                need_nth(pe, t, "prob_t", HEADS - 1, HEADS)
                pe.transpose(T[0:HEADS, 0:P], row_rec[:], c.ident[:]).then_inc(sem("rec_turned"), 1)

            def att_wide(t):
                need(pe, t, "rec_t")
                widen(T, rec_t).then_inc(sem("rec_wide"), 1)

            def att_norm(t):
                need(pe, t, "att_squared")
                for k in range(CT):
                    last = pe.matmul(T[:, N512:N512 + P], c.every[:], att_squares[:, k * P:(k + 1) * P], start=k == 0,
                                     stop=k == CT - 1)
                last.then_inc(sem("att_summed"), 1)

            steps = {"lora": lora, "key_sum": key_sum, "key_norm": key_norm, "turn0": turn0, "turn1": turn1,
                     "pairs": pairs, "center": center, "variance": variance, "gate": gate_y, "xa_rows": xa_rows,
                     "xa_query": xa_query, "xa_turn": xa_turn, "xa_score": xa_score, "xa_weigh": xa_weigh,
                     "xa_read": xa_read, "xa_out": xa_out, "ffn_turn": ffn_turn, "route": route,
                     "att_rec": att_rec, "att_wide": att_wide, "att_norm": att_norm}
            steps |= {f"cross{n}": cross_products(n) for n in range(1, LV + 1)}
            steps |= {f"grow{n}": grow(n) for n in range(1, LV + 1)}
            for p in range(2):
                steps |= {f"target{p}": solve_target(p), f"solve{p}": solve(p), f"output{p}": output(p)}
            steps |= {f"join{n}": join(n) for n in range(4)} | {f"head{h}": head(h) for h in range(HEADS + 2)}
            run(pe, steps)

        @block.scalar
        def _(act):
            def function(t, name, out, in_, func, needs=(), frees=(), **more):
                freed(act, t, *frees)
                need(act, t, *needs)
                act.activation(out, in_, func, **more).then_inc(sem(name), 1)

            def copy(t, name, out, in_, needs=(), frees=()):
                freed(act, t, *frees)
                need(act, t, *needs)
                act.copy(out, in_).then_inc(sem(name), 1)

            def inverse_root(t, name, logged, rstd, in_, scale, eps, needs, frees):
                function(t, f"{name}_logged", logged, in_, ACT.Ln, needs, scale=scale, bias=eps)
                function(t, f"{name}_rstd", rstd, logged, ACT.Exp, (f"{name}_logged",), frees, scale=-0.5)

            def lora(t):
                act.preload_act_table_set("exp_and_others")
                function(t, "tanh_w", lora_in[:], wag[0:LORA, 0, :], ACT.Tanh, ("wag_in",), ("lora_w",))
                function(t, "tanh_g", gate_half[:], wag[:, 1, :], ACT.Tanh, (), ("gate_in",), scale=0.5)

            def decay(t):
                function(t, "tanh_zw", decay_path[:], decay_path[:], ACT.Tanh, ("z_w",), scale=0.5)
                function(t, "tanh_za", iclr_path[:], iclr_path[:], ACT.Tanh, ("z_a",), scale=0.5)
                act.preload_act_table_set("natural_log_exp_and_others")
                function(t, "decayed", decayed[:], sum_path[:], ACT.Exp, ("decay_sum",), ("state1", "r_tilde"))
                function(t, "decayed_before", decay_path[:], decay_path[:], ACT.Exp, ("decay_before",))
                function(t, "grown", sum_path[:], sum_path[:], ACT.Exp, (), (), scale=-1.0)

            def key_sum(t):
                function(t, "kk_squared", rw_squares[:], kk[:], ACT.Square, ("kk_raw",), ("y_var",))

            def key_norm(t):
                function(t, "kk_logged", head_sum[:], head_sum[:], ACT.Ln, ("kk_floor",), scale=2.0 ** 20)
                function(t, "kk_rstd", head_rstd[:], head_sum[:], ACT.Exp, ("kk_logged",), ("y_wide",), scale=-0.5,
                         bias=m.shift_back[:, 0:1])

            def keep_rows(t, rows, bank, name):
                freed(act, t, "state_sum0")
                need(act, t, f"turned_{name}")
                for half in HALVES:
                    last = act.copy(rows[half, 0], tiles(bank)[HALVES[0], :, half])
                last.then_inc(sem(f"{name}_rows0"), 1)

            def turn0(t):
                keep_rows(t, v_rows, R2, "v")
                keep_rows(t, b_rows, R1, "b")

            def turn1(t):
                keep_rows(t, k_rows, R0, "k")

            def keep_target(p):
                def step(t):
                    copy(t, f"target_kept{p}", target[:], tiles((R1, R2)[p][:, 0:CT * HD], HD), (f"target{p}",),
                         ("solved1",) if p == 0 else ())
                return step

            def center(t):
                copy(t, "y_kept", y[:], tiles(R0), ("y_done1",), ("y_bonus",))
                function(t, "y_square", rw_squares[:], y_center[:], ACT.Square, ("y_center",))

            def variance(t):
                inverse_root(t, "y", head_sum[:], head_rstd[:], R2[0:HEADS, 0:P], 1.0 / HD, c.lnx_eps[0:HEADS, 0:1],
                             ("y_var", "kk_rstd"), ())

            def xa_norm(t):
                function(t, "x2_squared", normed[:], x_now[:], ACT.Square, ("x2",), ("h_out", "h_ffn_turned"),
                         accum_out=x2_sum[:])
                inverse_root(t, "x2", x2_logged[:], x2_rstd[:], x2_sum[:], 1.0 / DM, c.eps[:, 0:1], ("x2_squared",),
                             ("x2_scaled",))

            def xa_query(t):
                need_nth(act, after(t), "read", HEADS - 1, HEADS)
                function(t, "xq_squared", xq_normed, V, ACT.Square, ("xq",))
                inverse_root(t, "xq", xq_logged[:], xq_rstd[:], xq_sum[:], 1.0 / XD, c.eps[:, 0:1], ("xq_summed",),
                             ("xq_normed",))

            def xa_exp(t):
                freed(act, t, "xp_rstd")
                need(act, t, "xs_negmax")
                for h in range(XH):
                    last = act.activation(xp[:, h, :], S[:, h * N_MEM:(h + 1) * N_MEM], ACT.Exp,
                                          bias=xs_negmax[:, h:h + 1], accum_out=xp_sum[:, h:h + 1])
                last.then_inc(sem("xp"), 1)

            def xa_weigh(t):
                copy(t, "xp_t", xp_t, tiles(T), ("xp_turned",))

            def ffn_norm(t):
                function(t, "x3_squared", normed[:], x_now[:], ACT.Square, ("x3", "x2_turned"), (),
                         accum_out=x3_sum[:])
                inverse_root(t, "x3", x3_logged[:], x3_rstd[:], x3_sum[:], 1.0 / DM, c.eps[:, 0:1], ("x3_squared",),
                             ("h_ffn",))
                act.dma_start(dram["x3"][bass.ds(t * P, P), :], x_now[:]).then_inc(sem("x3_out"), 16)

            def ffn_turn(t):
                need(act, t, "h_ffn")
                act.dma_start(dram["h_ffn"][bass.ds(t * P, P), :], normed[:]).then_inc(sem("h_out"), 16)

            def head(h):
                def step(t):
                    if 1 <= h <= HEADS:
                        g = h - 1
                        need_nth(act, t, "score_neg", g, HEADS)
                        if g == 0:
                            freed(act, t, "att_rec")
                        act.activation(score[g % 2], score[g % 2], ACT.Exp, scale=-1.0,
                                       bias=neg_max[:, g:g + 1], accum_out=row_sum[:, g:g + 1]).then_inc(
                            sem("prob"), 1)
                    if h >= 2:
                        g = h - 2
                        need_nth(act, t, "read", g - 2, HEADS)
                        if g < 2:
                            tail_before(act, t, "xo_done")
                        need_nth(act, t, "prob_turned", g, HEADS)
                        act.copy(prob_t[g % 2], T[:, 0:BAND]).then_inc(sem("prob_t"), 1)
                return step

            def att_rec(t):
                need_nth(act, t, "read", HEADS - 1, HEADS)
                copy(t, "att_raw", att_y[:], tiles(V), (), ("att_t",))
                copy(t, "rec_t", rec_t, T[0:HEADS, 0:P], ("rec_turned",))

            def att_wide(t):
                function(t, "att_squared", att_squares, att_y[:].rearrange("p c n -> p (c n)"), ACT.Square,
                         ("att_y",))

            def att_norm(t):
                inverse_root(t, "att", att_rstd, att_rstd, T[:, N512:N512 + P], 1.0 / RW, c.eps[:, 0:1],
                             ("att_summed",), ())

            steps = {"lora": lora, "decay": decay, "key_sum": key_sum, "key_norm": key_norm, "turn0": turn0, "turn1": turn1,
                     "target0": keep_target(0), "target1": keep_target(1), "center": center, "variance": variance,
                     "xa_norm": xa_norm, "xa_query": xa_query, "xa_exp": xa_exp, "xa_weigh": xa_weigh,
                     "ffn_norm": ffn_norm, "ffn_turn": ffn_turn, "att_rec": att_rec, "att_wide": att_wide,
                     "att_norm": att_norm}
            steps |= {f"head{h}": head(h) for h in range(HEADS + 2)}
            run(act, steps)

        @block.vector
        def _(dve):
            def combine(t, name, out, in0, in1, op, needs=(), frees=()):
                freed(dve, t, *frees)
                need(dve, t, *needs)
                dve.tensor_tensor(out, in0, in1, op).then_inc(sem(name), 1)

            def scale(t, name, out, in0, one, two, op0, op1, needs=(), frees=()):
                freed(dve, t, *frees)
                need(dve, t, *needs)
                if op1 is None:
                    dve.tensor_scalar(out, in0, one, None, op0).then_inc(sem(name), 1)
                else:
                    dve.tensor_scalar(out, in0, one, two, op0, op1).then_inc(sem(name), 1)

            def lora(t):
                scale(t, "gate_in", gate_in[:], gate_half[:], 0.5, 0.5, ALU.mult, ALU.add, ("tanh_g",), ("lora_g",))

            def decay(t):
                combine(t, "z_w", decay_path[:], tiles(R0), spread(m.w0[:], P), ALU.add, ("lora_w",), ("a_tilde",))
                combine(t, "z_a", iclr_path[:], tiles(R1), spread(m.a0[:], P), ALU.add, ("lora_a",), ("bonus_done",))
                scale(t, "log_decay", decay_path[:], decay_path[:], -HALF_E, -HALF_E, ALU.mult, ALU.add,
                      ("tanh_zw",))
                need(dve, t, "log_decay")
                dve.tensor_tensor_scan(sum_path[:].rearrange("p c n -> p (c n)"), c.within[:],
                                       decay_path[:].rearrange("p c n -> p (c n)"), 0.0, ALU.mult,
                                       ALU.add).then_inc(sem("decay_sum"), 1)
                combine(t, "decay_before", decay_path[:], sum_path[:], decay_path[:], ALU.subtract,
                        ("decay_sum",))

            def key_sum(t):
                scale(t, "kk_floor", head_sum[:], R0[0:HEADS, 0:P], 1e-24, None, ALU.max, None, ("kk_sum",),
                      ("y_rstd",))

            def weigh(t):
                combine(t, "kk", kk[:], kk[:], tiles(R1), ALU.mult, ("kk_wide",))
                scale(t, "a_now", kk_a[:], iclr_path[:], 0.5, 0.5, ALU.mult, ALU.add, ("tanh_za",))
                combine(t, "kk_a", kk_a[:], kk[:], kk_a[:], ALU.mult, ("kk", "a_now"))
                need(dve, t, "decayed_before")
                freed(dve, t, "y_done1")
                dve.scalar_tensor_tensor(out=a_and_r[:, :, :, 0], in0=by_chunk(kk), scalar=-1.0,
                                         in1=by_chunk(decay_path),
                                         op0=ALU.mult, op1=ALU.mult).then_inc(sem("a_tilde"), 1)
                combine(t, "b_tilde", b_tilde[:], kk_a[:], sum_path[:], ALU.mult, ("kk_a", "grown"))
                for k in range(CT):
                    last = dve.tensor_scalar(iclr_path[:, k, :], iclr_path[:, k, :], m.half_k_a[:, k:k + 1],
                                             m.rest_k_a[:, k:k + 1], ALU.mult, ALU.add)
                last.then_inc(sem("k_weight"), 1)
                combine(t, "k_new", iclr_path[:], rk[:, 1], iclr_path[:], ALU.mult, ("k_weight",))
                combine(t, "k_tilde", k_tilde[:], iclr_path[:], sum_path[:], ALU.mult, ("k_new",))

            def copy(t, name, out, in_, needs=(), frees=()):
                freed(dve, t, *frees)
                need(dve, t, *needs)
                dve.tensor_copy(out, in_).then_inc(sem(name), 1)

            def keep_rows(t, rows, bank, name):
                freed(dve, t, "state_sum1")
                need(dve, t, f"turned_{name}")
                for half in HALVES:
                    last = dve.tensor_copy(rows[half, 1], tiles(bank)[HALVES[1], :, half])
                last.then_inc(sem(f"{name}_rows1"), 1)

            def turn0(t):
                keep_rows(t, v_rows, R2, "v")
                keep_rows(t, b_rows, R1, "b")

            def turn1(t):
                keep_rows(t, k_rows, R0, "k")

            def pairs(t):
                mask = per_head(c.level_mask[:, 0, :], PAIRS)
                combine(t, "p3_masked", inverse[:], tiles(R2, HD), mask, ALU.mult, ("p3_done",))
                combine(t, "inverse", inverse[:], inverse[:], per_head(c.ident_half[:], PAIRS), ALU.add,
                        ("p3_masked",))
                for p, bank in enumerate((R0, R1)):
                    combine(t, f"p1_kept{p}", from_b[:, p * CT:(p + 1) * CT], tiles(bank), per_head(c.causal[:], CT),
                            ALU.mult, (f"p1_done{p}",))

            def first_level(t):
                combine(t, "first_t", inverse_t[:], from_b[:, :, 0:HD], per_head(c.level_mask_t[:, 0, :], PAIRS),
                        ALU.mult, ("p1_kept1",))
                combine(t, "inverse_t", inverse_t[:], inverse_t[:], per_head(c.ident_half[:], PAIRS), ALU.add,
                        ("first_t",))
                for p, bank in enumerate((R2, R0)):
                    combine(t, f"p2_kept{p}", from_k[:, p * CT:(p + 1) * CT], tiles(bank), per_head(c.causal[:], CT),
                            ALU.mult, (f"p2_done{p}",))

            def keep_cross(n):
                def step(t):
                    need_nth(dve, t, "cross_done", n - 1, LV)
                    dve.tensor_tensor(cross[:], tiles(R1, HD), per_head(c.level_mask[:, n, :], PAIRS),
                                      ALU.mult).then_inc(sem("cross_kept"), 1)
                return step

            def grow(n):
                def step(t):
                    need_nth(dve, t, "grow_t_done", n - 1, LV)
                    if n < LV:
                        dve.tensor_tensor(inverse[:], tiles(R2, HD), inverse[:], ALU.add).then_inc(
                            sem("inverse_new"), 1)
                    dve.tensor_tensor(inverse_t[:], tiles(R0, HD), inverse_t[:], ALU.add).then_inc(
                        sem("inverse_t_new"), 1)
                return step

            def keep_u(p):
                def step(t):
                    copy(t, f"u{p}", u[:], tiles((R2, R1)[p][:, 0:CT * HD], HD), (f"solved{p}",)
                         + (("state_sum0",) if p else ()))
                return step

            def add_state(p):
                def step(t):
                    combine(t, f"state_added{p}", state_sum[:], tiles((R1, R2)[p][:, 0:CT * HD], HD), m.state[:],
                            ALU.add, (f"state_sum{p}",))
                    at = (p + 1) * CHUNK - 1
                    combine(t, f"state{p}", m.state[:], state_sum[:],
                            decayed[:, :, at:at + 1].broadcast_to([P, CT, HD]), ALU.mult, (f"state_added{p}",))
                return step

            def center(t):
                need(dve, t, "y_mean")
                freed(dve, t, "y_square")
                dve.scalar_tensor_tensor(out=y_center[:], in0=tiles(R1), scalar=-1.0 / HD, in1=y[:], op0=ALU.mult,
                                         op1=ALU.add).then_inc(sem("y_center"), 1)

            def variance(t):
                combine(t, "bonus_v", y[:], tiles(R0), v_now[:], ALU.mult, ("bonus_done", "y_center"))

            def gate_y(t):
                combine(t, "y_norm", y_center[:], tiles(R1), y_center[:], ALU.mult, ("y_wide",))
                need(dve, t, "y_norm")
                for k in range(CT):
                    last = dve.tensor_scalar(y_center[:, k, :], y_center[:, k, :], m.ln_w[:, k:k + 1],
                                             m.ln_b[:, k:k + 1], ALU.mult, ALU.add)
                last.then_inc(sem("y_affine"), 1)
                combine(t, "y_bonus", y[:], y_center[:], y[:], ALU.add, ("y_affine", "bonus_v"))
                combine(t, "y_out", y_out[:], tiles(R2), y[:], ALU.mult, ("y_bonus", "lora_g"), ("joined",))

            def join3(t):
                combine(t, "x2", x_now[:], S, x_now[:], ALU.add, ("joined", "x_in"))

            def xa_norm(t):
                scale(t, "x2_scaled", normed[:], x_now[:], x2_rstd[:, 0:1], None, ALU.mult, None, ("x2_rstd",))

            def xa_rows(t):
                combine(t, "hx", normed_t[:], tiles(T), spread(m.gain_xa[:], P), ALU.mult, ("x2_turned",),
                        ("logits_done",))

            def xa_query(t):
                need(dve, t, "xq_squared")
                freed(dve, t, "xq_logged")
                dve.tensor_reduce(xq_sum[:], xq_normed.rearrange("p (h d) -> p h d", d=XD), AX.X,
                                  ALU.add).then_inc(sem("xq_summed"), 1)
                combine(t, "xq_normed", xq_normed.rearrange("p (h d) -> p h d", d=XD), tiles(V),
                        spread(xq_rstd[:], XD), ALU.mult, ("xq_rstd",))

            def xa_turn(t):
                scale(t, "xq_t", xqo_t[:], tiles(T[:, 0:XW]), m.scaled_q[:, 0:1], None, ALU.mult, None,
                      ("xq_turned",), ())

            def xa_score(t):
                need(dve, t, "xs_done")
                dve.tensor_reduce(xs_max[:], tiles(S, N_MEM), AX.X, ALU.max).then_inc(sem("xs_max"), 1)
                scale(t, "xs_negmax", xs_negmax[:], xs_max[:], -1.0, None, ALU.mult, None, ("xs_max",), ("xp",))

            def xa_exp(t):
                need(dve, t, "xp")
                dve.reciprocal(xp_rec[:], xp_sum[:]).then_inc(sem("xp_rstd"), 1)
                combine(t, "xp_normed", xp, xp, spread(xp_rec[:], N_MEM), ALU.mult, ("xp_rstd",))

            def xa_read(t):
                copy(t, "xo_t", xqo_t[:], tiles(V), ("xo_done", "xs_done"))

            def xa_out(t):
                combine(t, "x3", x_now[:], S, x_now[:], ALU.add, ("xout",))

            def ffn_norm(t):
                scale(t, "h_ffn", normed[:], x_now[:], x3_rstd[:, 0:1], None, ALU.mult, None, ("x3_rstd",))

            def ffn_turn(t):
                combine(t, "h_ffn_t", normed_t[:], tiles(T), spread(m.gain_ffn[:], P), ALU.mult,
                        ("h_ffn_turned", "xq"))

            def route(t):
                need(dve, t, "logits_done")
                dve.tensor_tensor(m.logits[:, bass.ds(t, 1), :].rearrange("p o n -> p (o n)"), V[:, 0:LOGITS],
                                  m.b_router[:], ALU.add).then_inc(sem("logits"), 1)

            def head(h):
                def step(t):
                    if h == 0:
                        freed(dve, t, "bias_in")
                        tail_before(dve, t, "xp_turned")
                    need_nth(dve, t, "prob_turned", h - 2, HEADS)
                    need_nth(dve, t, "scores", h, HEADS, alone=True)
                    dve.tensor_tensor_reduce(out=score[h % 2], in0=S[:, 0:BAND], in1=m.bias[:, h, :], scale=-1.0,
                                             scalar=3e38, op0=ALU.add, op1=ALU.min,
                                             accum_out=neg_max[:, h:h + 1]).then_inc(sem("score_neg"), 1)
                return step

            def att_rec(t):
                need_nth(dve, t, "prob", HEADS - 1, HEADS)
                freed(dve, t, "rec_turned")
                dve.reciprocal(row_rec[:], row_sum[:]).then_inc(sem("att_rec"), 1)

            def att_wide(t):
                combine(t, "att_y", att_y[:], tiles(T[:, 0:RW]), att_y[:], ALU.mult, ("rec_wide", "att_raw"))

            def att_norm(t):
                combine(t, "att_scaled", att_y[:], att_y[:], per_head(att_rstd, CT), ALU.mult, ("att_rstd",))

            def att_gain(t):
                combine(t, "att_t", att_t[:], att_y[:], spread(m.gain_att[:], P), ALU.mult, ("att_scaled",),
                        ("xout",))

            steps = {"lora": lora, "decay": decay, "key_sum": key_sum, "weigh": weigh, "turn0": turn0,
                     "turn1": turn1, "pairs": pairs, "first_level": first_level, "center": center,
                     "variance": variance, "gate": gate_y, "join3": join3, "xa_norm": xa_norm,
                     "xa_rows": xa_rows, "xa_query": xa_query, "xa_turn": xa_turn, "xa_score": xa_score,
                     "xa_exp": xa_exp, "xa_read": xa_read,
                     "xa_out": xa_out, "ffn_norm": ffn_norm, "ffn_turn": ffn_turn, "route": route,
                     "att_rec": att_rec, "att_wide": att_wide, "att_norm": att_norm, "att_gain": att_gain}
            steps |= {f"cross{n}": keep_cross(n) for n in range(1, LV + 1)}
            steps |= {f"grow{n}": grow(n) for n in range(1, LV + 1)}
            for p in range(2):
                steps |= {f"solve{p}": keep_u(p), f"output{p}": add_state(p)}
            steps |= {f"head{h}": head(h) for h in range(HEADS)}
            run(dve, steps)

        @block.gpsimd
        def _(pool):
            def combine(t, name, out, in0, in1, op, needs=(), frees=()):
                freed(pool, t, *frees)
                need(pool, t, *needs)
                pool.tensor_tensor(out, in0, in1, op).then_inc(sem(name), 1)

            def key_sum(t):
                combine(t, "kk_raw", kk[:], rk[:, 1], spread(m.gain_kk[:], P), ALU.mult, ("rk_in",),
                        ("a_tilde",))

            def weigh(t):
                combine(t, "r_tilde", a_and_r[:, :, :, 1], by_chunk(rk[:, 0]), by_chunk(decayed), ALU.mult,
                        ("decayed",), ("y_done1",))
                combine(t, "r_k_raw", iclr_path[:], rk[:, 0], iclr_path[:], ALU.mult, ("k_tilde",))
                combine(t, "r_k_pair", iclr_path[:], iclr_path[:], spread(m.r_k[:], P), ALU.mult, ("r_k_raw",))

            run(pool, {"key_sum": key_sum, "weigh": weigh})


def route_tokens(nc, a, c, r, dram, banks):
    with ExitStack() as stack:
        sb = Memory(nc, stack, "route")
        sem = Signals(nc, stack, "route")
        token = sb("token", P, TILES, dt=I32)
        empty = sb("empty", P, BLOCKS, dt=I32)
        index = sb("index", P, PER_GROUP)
        index_low = sb("index_low", P, PER_GROUP)
        block_first = sb("block_first", P, TILES)
        block = sb("block", 1, BLOCKS)
        earlier = sb("earlier", P, P)
        every = sb("every", P, P)
        group_shift, group_exp, group_one = (sb(n, P, TILES, GROUPS) for n in (
            "group_shift", "group_exp", "group_one"))
        gate = sb("gate", P, TILES)
        one_value = sb("one_value", P, TILES)
        by_group = sb("by_group", P, TILES, GROUPS, PER_GROUP)
        chosen, equal = sb("chosen", P, TILES, PER_GROUP), sb("equal", P, TILES, PER_GROUP)
        one_hot = [sb(f"one_hot{j}", P, TILES, PER_GROUP) for j in range(2)]
        best = [sb(f"best{j}", P, TILES) for j in range(2)]
        expert_hot = [sb(f"expert_hot{j}", P, TILES, EXPERTS) for j in range(2)]
        both_hot, before, slot_all, product = (sb(n, P, TILES, EXPERTS) for n in (
            "both_hot", "before", "slot_all", "product"))
        count, blocks_of, blocks_end, first_slot = (sb(n, P, EXPERTS) for n in (
            "count", "blocks_of", "blocks_end", "first_slot"))
        over = sb("over", P, EXPERTS, TILES)
        slot = sb("slot", P, 2, TILES)
        ended = sb("ended", 1, BLOCKS, EXPERTS)
        expert, half_total, turn_used = sb("expert", 1, BLOCKS), sb("half_total", 1, 1), sb("turn_used", 1, BLOCKS // 2)
        FAR = 64.0
        in_tile, per_tile = banks[:, 0], banks[:, 1]
        code = stack.enter_context(nc.Block())

        @code.gpsimd
        def _(pool):
            made = [0]

            def then(instruction):
                instruction.then_inc(sem("tables"), 1)
                made[0] += 1
                pool.wait_ge(sem("tables"), made[0])

            then(pool.iota(token[:], [[P, TILES]], base=0, channel_multiplier=1))
            then(pool.memset(empty[:], 0))
            then(pool.iota(index[:], [[1, PER_GROUP]], base=0, channel_multiplier=0,
                           allow_small_or_imprecise_dtypes=True))
            then(pool.iota(index_low[:], [[1, PER_GROUP]], base=-int(FAR), channel_multiplier=0,
                           allow_small_or_imprecise_dtypes=True))
            then(pool.iota(block_first[:], [[P, TILES]], base=0, channel_multiplier=0,
                           allow_small_or_imprecise_dtypes=True))
            then(pool.iota(block[:], [[1, BLOCKS]], base=0, channel_multiplier=0,
                           allow_small_or_imprecise_dtypes=True))
            then(pool.memset(every[:], 1.0))
            then(pool.affine_select(out=earlier[:], in_=every[:], compare_op=ALU.is_ge, fill=0.0, base=-1,
                                    pattern=[[1, P]], channel_multiplier=-1))
            pool.sem_inc(sem("tables_set"), 1)
            pool.dma_start(dram["slot_token"].rearrange("(p n) o -> p (n o)", p=P), empty[:]).then_inc(
                sem("emptied"), 16)
            pool.wait_ge(sem("emptied"), 16)
            pool.wait_ge(sem("slot_of"), 1)
            for t in range(TILES):
                for j in range(2):
                    pool.indirect_dma_start(
                        out=dram["slot_token"], out_offset=bass.IndirectOffsetOnAxis(ap=r.slot_of[:, t, j:j + 1],
                                                                                     axis=0),
                        in_=token[:, t:t + 1], in_offset=None).then_inc(sem("slots_out"), 16)
            pool.wait_ge(sem("slots_out"), 16 * 2 * TILES)

        @code.scalar
        def _(act):
            act.preload_act_table_set("natural_log_exp_and_others")
            act.wait_ge(sem("group_shift"), 1)
            act.activation(group_exp[:], group_shift[:], ACT.Exp).then_inc(sem("group_exp"), 1)
            act.wait_ge(sem("second_less_first"), 1)
            act.activation(one_value[:], one_value[:], ACT.Exp).then_inc(sem("ratio"), 1)

        @code.sync
        def _(sp):
            with nc.allow_non_contiguous_dma(reason="a gain vector over partitions"):
                sp.dma_start(r.gain[:], column(a["norm_ffn"][0], KT)).then_inc(sem("gain_in"), 16)
            sp.wait_ge(sem("gain_in"), 16)

        @code.tensor
        def _(pe):
            pe.wait_ge(sem("both_hot"), 1)
            rows = both_hot[:].rearrange("p t e -> p (t e)")
            pe.matmul(in_tile, earlier[:], rows, start=True, stop=True).then_inc(sem("counted"), 1)
            pe.matmul(per_tile, every[:], rows, start=True, stop=True).then_inc(sem("counted"), 1)

        @code.vector
        def _(dve):
            made = [0]

            def then(instruction, name="step"):
                instruction.then_inc(sem(name), 1)
                if name == "step":
                    made[0] += 1
                    dve.wait_ge(sem("step"), made[0])
                else:
                    dve.wait_ge(sem(name), 1)

            def first_greatest(values, greatest, hot, n):
                eq = equal[:, :, 0:n]
                then(dve.tensor_reduce(greatest, values, AX.X, ALU.max))
                then(dve.tensor_tensor(eq, values, spread(greatest, n), ALU.is_equal))
                then(dve.scalar_tensor_tensor(out=eq, in0=eq, scalar=-FAR, in1=per_head(index[:, 0:n], TILES),
                                              op0=ALU.mult, op1=ALU.add))
                then(dve.tensor_reduce(one_value[:], eq, AX.X, ALU.min))
                then(dve.tensor_tensor(hot, per_head(index_low[:, 0:n], TILES), spread(one_value[:], n),
                                       ALU.is_equal))

            dve.wait_ge(sem("tables_set"), 1)
            of_groups = r.logits[:, :, 0:GROUPS]
            first_greatest(of_groups, gate[:], group_one[:], GROUPS)
            then(dve.tensor_tensor(group_shift[:], of_groups, spread(gate[:], GROUPS), ALU.subtract), "group_shift")
            dve.wait_ge(sem("group_exp"), 1)
            then(dve.tensor_reduce(one_value[:], group_exp[:], AX.X, ALU.add))
            then(dve.reciprocal(gate[:], one_value[:]))
            for g in range(GROUPS):
                of_group = r.logits[:, :, GROUPS + g * PER_GROUP:GROUPS + (g + 1) * PER_GROUP]
                then(dve.tensor_tensor(by_group[:, :, g, :], of_group, group_one[:, :, g:g + 1].broadcast_to(
                    [P, TILES, PER_GROUP]), ALU.mult))
            then(dve.tensor_tensor(chosen[:], by_group[:, :, 0, :], by_group[:, :, 1, :], ALU.add))
            then(dve.tensor_tensor(chosen[:], chosen[:], by_group[:, :, 2, :], ALU.add))
            then(dve.tensor_tensor(chosen[:], chosen[:], by_group[:, :, 3, :], ALU.add))
            first_greatest(chosen[:], best[0][:], one_hot[0][:], PER_GROUP)
            then(dve.scalar_tensor_tensor(out=chosen[:], in0=one_hot[0][:], scalar=-3e38, in1=chosen[:],
                                          op0=ALU.mult, op1=ALU.add))
            first_greatest(chosen[:], best[1][:], one_hot[1][:], PER_GROUP)
            then(dve.tensor_tensor(one_value[:], best[1][:], best[0][:], ALU.subtract), "second_less_first")
            dve.wait_ge(sem("ratio"), 1)
            then(dve.tensor_scalar(best[0][:], one_value[:], 1.0, None, ALU.add))
            then(dve.reciprocal(best[1][:], best[0][:]))
            first, second = (r.weight[:, :, j:j + 1].rearrange("p t o -> p (t o)") for j in range(2))
            then(dve.tensor_tensor(first, gate[:], best[1][:], ALU.mult))
            then(dve.tensor_tensor(second, first, one_value[:], ALU.mult))
            for j in range(2):
                for g in range(GROUPS):
                    then(dve.tensor_tensor(expert_hot[j][:, :, g * PER_GROUP:(g + 1) * PER_GROUP], one_hot[j][:],
                                           group_one[:, :, g:g + 1].broadcast_to([P, TILES, PER_GROUP]), ALU.mult))
            then(dve.tensor_tensor(both_hot[:], expert_hot[0][:], expert_hot[1][:], ALU.add), "both_hot")
            dve.wait_ge(sem("counted"), 2)
            totals = per_tile.rearrange("p (t e) -> p t e", e=EXPERTS)
            then(dve.memset(before[:, 0, :], 0.0))
            for t in range(1, TILES):
                then(dve.tensor_tensor(before[:, t, :], before[:, t - 1, :], totals[:, t - 1, :], ALU.add))
            then(dve.tensor_tensor(count[:], before[:, TILES - 1, :], totals[:, TILES - 1, :], ALU.add))
            then(dve.tensor_tensor(over[:], spread(count[:], TILES), per_head(block_first[:], EXPERTS), ALU.is_gt))
            then(dve.tensor_reduce(blocks_of[:], over[:], AX.X, ALU.add))
            then(dve.tensor_tensor_scan(blocks_end[:], every[:, 0:EXPERTS], blocks_of[:], 0.0, ALU.mult, ALU.add))
            then(dve.tensor_tensor(first_slot[:], blocks_end[:], blocks_of[:], ALU.subtract))
            then(dve.tensor_scalar(first_slot[:], first_slot[:], float(P), None, ALU.mult))
            then(dve.tensor_tensor(slot_all[:], in_tile.rearrange("p (t e) -> p t e", e=EXPERTS), before[:],
                                   ALU.add))
            then(dve.tensor_tensor(slot_all[:], slot_all[:], per_head(first_slot[:], TILES), ALU.add))
            for j in range(2):
                then(dve.tensor_tensor(product[:], expert_hot[j][:], slot_all[:], ALU.mult))
                then(dve.tensor_reduce(slot[:, j, :], product[:], AX.X, ALU.add))
            then(dve.tensor_copy(r.slot_of[:], slot[:].rearrange("p j t -> p t j")), "slot_of")
            then(dve.tensor_tensor(ended[:], per_head(blocks_end[0:1, :], BLOCKS), spread(block[:], EXPERTS),
                                   ALU.is_le))
            then(dve.tensor_reduce(expert[:], ended[:], AX.X, ALU.add))
            then(dve.tensor_scalar(expert[:], expert[:], EXPERTS - 1.0, None, ALU.min))
            then(dve.tensor_copy(r.expert_of[:], expert[:]))
            then(dve.tensor_scalar(half_total[:], blocks_end[0:1, EXPERTS - 1:EXPERTS], 0.5, None, ALU.mult))
            then(dve.tensor_tensor(turn_used[:], half_total[:].broadcast_to([1, BLOCKS // 2]),
                                   block[:, 0:BLOCKS // 2], ALU.is_gt))
            then(dve.tensor_reduce(half_total[:], turn_used[:], AX.X, ALU.add))
            then(dve.tensor_copy(r.turns[:], half_total[:]))


def run_experts(nc, a, c, r, dram, banks):
    with ExitStack() as stack:
        sb = Memory(nc, stack, "expert")
        both = lambda *names: " ".join(f"{n}{half}" for n in names for half in range(2))
        sem = Signals(nc, stack, "expert", both("turned", "x_t", "gate_done", "up_done", "exped", "plus_one", "sigmoid", "silu",
                                                "hidden", "hidden_turned", "hidden_t") + " "
                      + both("y_done0_", "y_done1_", "y_kept0_", "y_kept1_"),
                      both("ids_in", "w_gate_in", "w_up_in", "w_down_in", "y_out"))
        nc.gpsimd.sem_inc(sem("begun"), 1)
        w_gate, w_up = ([sb(f"{n}{half}", P, KT, FF) for half in range(2)] for n in ("w_gate", "w_up"))
        w_down = [sb(f"w_down{half}", P, FT, DM) for half in range(2)]
        zeros = sb("zeros", P, DM)
        ids = [sb(f"ids{half}", P, 1, dt=I32) for half in range(2)]
        rows = [sb(f"rows{half}", P, DM) for half in range(2)]
        x_t = [sb(f"x_t{half}", P, KT, P) for half in range(2)]
        sigmoid, hidden = ([sb(f"{n}{half}", P, FF) for half in range(2)] for n in ("sigmoid", "hidden"))
        hidden_t = [sb(f"hidden_t{half}", P, FT, P) for half in range(2)]
        y = [sb(f"y{half}", P, DM) for half in range(2)]
        turned = banks[:, 0:2].rearrange("p b n -> p (b n)")
        gate, up, hidden_turned, y_bank = [banks[:, 2], banks[:, 3]], banks[:, 4], banks[:, 5], [banks[:, 6], banks[:, 7]]
        block = stack.enter_context(nc.Block())
        TURNS = BLOCKS // 2

        def turns_used(engine):
            return engine.value_load(r.turns[0:1, 0:1], min_val=1, max_val=TURNS)

        @block.sync
        def _(sp):
            used = turns_used(sp)
            with sp.Fori(0, TURNS) as i:
                with sp.If(i < used):
                    for half in range(2):
                        sp.wait_ge(sem(f"turned{half}"), i + 1)
                        sp.dma_start(ids[half][:], dram["slot_token"][bass.ds((2 * i + half) * P, P), :]).then_inc(
                            sem(f"ids_in{half}"), 16)
                    for half in range(2):
                        e = sp.value_load(r.expert_of[0:1, bass.ds(2 * i + half, 1)], min_val=0, max_val=EXPERTS - 1)
                        for w, name in ((w_gate, "gate"), (w_up, "up"), (w_down, "down")):
                            sp.wait_ge(sem(f"y_done1_{half}" if name == "down" else f"{name}_done{half}"), i + 1)
                            sp.dma_start(w[half][:], a[f"moe_w_{name}"][0, bass.ds(e, 1)].rearrange(
                                "o (k p) n -> p (o k) n", p=P)).then_inc(sem(f"w_{name}_in{half}"), 16)
            for half in range(2):
                sp.wait_ge(sem(f"y_out{half}"), 16 * (TURNS + 1))

        @block.gpsimd
        def _(pool):
            pool.memset(zeros[:], 0.0).then_inc(sem("zeros_set"), 1)
            before, count = pool.alloc_register("turned_before"), pool.alloc_register("ids_loaded")
            used = turns_used(pool)
            with pool.Fori(0, TURNS) as i:
                with pool.If(i < used):
                    for half in range(2):
                        pool.reg_mov(before, i + 1)
                        pool.reg_mov(count, 16 * i + 32)
                        pool.wait_ge(sem("begun"), 1)
                        pool.wait_ge(sem(f"turned{half}"), before)
                        pool.wait_ge(sem(f"ids_in{half}"), count)
                        pool.indirect_dma_start(
                            out=rows[half][:], out_offset=None, in_=dram["h_ffn"],
                            in_offset=bass.IndirectOffsetOnAxis(ap=ids[half][:, 0:1], axis=0)).then_inc(
                            sem(f"rows_in{half}"), 16)

        @block.scalar
        def _(act):
            act.preload_act_table_set("natural_log_exp_and_others")
            act.wait_ge(sem("zeros_set"), 1)

            def exp(i, half):
                act.wait_ge(sem(f"silu{half}"), i + 1)
                act.wait_ge(sem(f"gate_done{half}"), i + 2)
                act.activation(sigmoid[half][:], gate[half], ACT.Exp, scale=-1.0).then_inc(sem(f"exped{half}"), 1)

            def turn(i, half):
                act.wait_ge(sem(f"y_done1_{half}"), i + 1)
                act.wait_ge(sem(f"hidden_turned{half}"), i + 2)
                act.copy(hidden_t[half][:], hidden_turned.rearrange("p (f n) -> p f n", n=P)).then_inc(
                    sem(f"hidden_t{half}"), 1)

            def keep(i, half):
                act.wait_ge(sem(f"y_out{half}"), 16 * i + 16)
                for n in range(2):
                    act.wait_ge(sem(f"y_done{n}_{half}"), i + 2)
                    act.copy(y[half][:, n * N512:(n + 1) * N512], y_bank[n]).then_inc(sem(f"y_kept{n}_{half}"), 1)
                act.wait_ge(sem(f"y_kept1_{half}"), i + 2)
                act.dma_start(dram["y"][bass.ds((2 * i + half) * P, P), :], y[half][:]).then_inc(
                    sem(f"y_out{half}"), 16)

            used = turns_used(act)
            with act.Fori(0, TURNS) as i:
                with act.If(i < used):
                    exp(i, 0)
                    exp(i, 1)
                    turn(i, 0)
                    keep(i, 0)
                    turn(i, 1)
                    keep(i, 1)
                with act.Else():
                    for half in range(2):
                        act.dma_start(dram["y"][bass.ds((2 * i + half) * P, P), :], zeros[:]).then_inc(
                            sem(f"y_out{half}"), 16)

        @block.vector
        def _(dve):
            def gain(i, half):
                dve.wait_ge(sem(f"up_done{half}"), i + 1)
                dve.wait_ge(sem(f"turned{half}"), i + 2)
                dve.tensor_tensor(x_t[half][:], turned.rearrange("p (k n) -> p k n", n=P), spread(r.gain[:], P),
                                  ALU.mult).then_inc(sem(f"x_t{half}"), 1)

            def silu(i, half):
                s = sigmoid[half][:]
                dve.wait_ge(sem(f"exped{half}"), i + 2)
                dve.tensor_scalar(s, s, 1.0, None, ALU.add).then_inc(sem(f"plus_one{half}"), 1)
                dve.wait_ge(sem(f"plus_one{half}"), i + 2)
                dve.reciprocal(s, s).then_inc(sem(f"sigmoid{half}"), 1)
                dve.wait_ge(sem(f"hidden_turned{half}"), i + 1)
                dve.wait_ge(sem(f"sigmoid{half}"), i + 2)
                dve.tensor_tensor(hidden[half][:], gate[half], s, ALU.mult).then_inc(sem(f"silu{half}"), 1)

            def hide(i, half):
                dve.wait_ge(sem(f"silu{half}"), i + 2)
                dve.wait_ge(sem(f"up_done{half}"), i + 2)
                dve.tensor_tensor(hidden[half][:], up, hidden[half][:], ALU.mult).then_inc(sem(f"hidden{half}"), 1)

            used = turns_used(dve)
            with dve.Fori(0, TURNS) as i:
                with dve.If(i < used):
                    gain(i, 0)
                    gain(i, 1)
                    silu(i, 0)
                    hide(i, 0)
                    silu(i, 1)
                    hide(i, 1)

        @block.tensor
        def _(pe):
            def turn_rows(i, half):
                pe.wait_ge(sem(f"x_t{1 - half}"), i + 1 + half)
                pe.wait_ge(sem(f"rows_in{half}"), 16 * i + 16)
                for k in range(KT):
                    last = pe.transpose(turned[:, k * P:(k + 1) * P], rows[half][:, k * P:(k + 1) * P], c.ident[:])
                last.then_inc(sem(f"turned{half}"), 1)

            def project(i, half, bank, w, name, *waits):
                for signal, count in waits:
                    pe.wait_ge(sem(signal), count)
                pe.wait_ge(sem(f"w_{name}_in{half}"), 16 * i + 32)
                for k in range(KT):
                    last = pe.matmul(bank, x_t[half][:, k, :], w[half][:, k, :], start=k == 0, stop=k == KT - 1)
                last.then_inc(sem(f"{name}_done{half}"), 1)

            def turn_hidden(i, half):
                pe.wait_ge(sem(f"hidden_t{1 - half}"), i + 1 + half)
                pe.wait_ge(sem(f"hidden{half}"), i + 2)
                for k in range(FT):
                    last = pe.transpose(hidden_turned[:, k * P:(k + 1) * P], hidden[half][:, k * P:(k + 1) * P],
                                        c.ident[:])
                last.then_inc(sem(f"hidden_turned{half}"), 1)

            def down(i, half):
                pe.wait_ge(sem(f"w_down_in{half}"), 16 * i + 32)
                pe.wait_ge(sem(f"hidden_t{half}"), i + 2)
                for n in range(2):
                    pe.wait_ge(sem(f"y_kept{n}_{1 - half}"), i + 1 + half)
                    for k in range(FT):
                        last = pe.matmul(y_bank[n], hidden_t[half][:, k, :], w_down[half][:, k, n * N512:(n + 1) * N512],
                                         start=k == 0, stop=k == FT - 1)
                    last.then_inc(sem(f"y_done{n}_{half}"), 1)

            used = turns_used(pe)
            with pe.Fori(0, TURNS) as i:
                with pe.If(i < used):
                    turn_rows(i, 0)
                    project(i, 0, gate[0], w_gate, "gate", ("silu0", i + 1), ("x_t0", i + 2))
                    turn_rows(i, 1)
                    project(i, 0, up, w_up, "up", ("hidden1", i + 1))
                    project(i, 1, gate[1], w_gate, "gate", ("silu1", i + 1), ("x_t1", i + 2))
                    turn_hidden(i, 0)
                    project(i, 1, up, w_up, "up", ("hidden0", i + 2))
                    down(i, 0)
                    turn_hidden(i, 1)
                    down(i, 1)


def combine_experts(nc, r, dram, out):
    with ExitStack() as stack:
        sb = Memory(nc, stack, "combine")
        SETS = 4
        each = lambda *names: " ".join(f"{n}{tile}" for n in names for tile in range(SETS))
        sem = Signals(nc, stack, "combine", each("ids", "first_added", "summed"), each("x_in", "out"))
        nc.gpsimd.sem_inc(sem("begun"), 1)
        x, first, second = ([sb(f"{n}{tile}", P, DM) for tile in range(SETS)] for n in ("x", "first", "second"))
        ids = [sb(f"ids{tile}", P, 2, dt=I32) for tile in range(SETS)]
        block = stack.enter_context(nc.Block())
        TURNS = TILES // SETS

        @block.sync
        def _(sp):
            with sp.Fori(0, TURNS) as i:
                for tile in range(SETS):
                    sp.wait_ge(sem(f"out{tile}"), 16 * i + 16)
                    sp.dma_start(x[tile][:], dram["x3"][bass.ds((SETS * i + tile) * P, P), :]).then_inc(
                        sem(f"x_in{tile}"), 16)

        @block.gpsimd
        def _(pool):
            before, count = pool.alloc_register("summed_before"), pool.alloc_register("ids_copied")
            with pool.Fori(0, TURNS) as i:
                for tile in range(SETS):
                    pool.reg_mov(before, i + 1)
                    pool.reg_mov(count, i + 2)
                    pool.wait_ge(sem("begun"), 1)
                    pool.wait_ge(sem(f"summed{tile}"), before)
                    pool.wait_ge(sem(f"ids{tile}"), count)
                    for j, rows in enumerate((first, second)):
                        pool.indirect_dma_start(
                            out=rows[tile][:], out_offset=None, in_=dram["y"],
                            in_offset=bass.IndirectOffsetOnAxis(ap=ids[tile][:, j:j + 1], axis=0)).then_inc(
                            sem(f"rows_in{j}_{tile}"), 16)

        @block.vector
        def _(dve):
            with dve.Fori(0, TURNS) as i:
                for tile in range(SETS):
                    dve.wait_ge(sem("begun"), 1)
                    dve.wait_ge(sem(f"summed{tile}"), i + 1)
                    dve.tensor_copy(ids[tile][:], r.slot_of[:, bass.ds(SETS * i + tile, 1), :].rearrange(
                        "p o j -> p (o j)")).then_inc(sem(f"ids{tile}"), 1)
                for tile in range(SETS):
                    weight = r.weight[:, bass.ds(SETS * i + tile, 1), :].rearrange("p o j -> p (o j)")
                    dve.wait_ge(sem(f"x_in{tile}"), 16 * i + 32)
                    dve.wait_ge(sem(f"rows_in0_{tile}"), 16 * i + 16)
                    dve.scalar_tensor_tensor(out=x[tile][:], in0=first[tile][:], scalar=weight[:, 0:1],
                                             in1=x[tile][:], op0=ALU.mult, op1=ALU.add).then_inc(
                        sem(f"first_added{tile}"), 1)
                    dve.wait_ge(sem(f"first_added{tile}"), i + 2)
                    dve.wait_ge(sem(f"rows_in1_{tile}"), 16 * i + 16)
                    dve.scalar_tensor_tensor(out=x[tile][:], in0=second[tile][:], scalar=weight[:, 1:2],
                                             in1=x[tile][:], op0=ALU.mult, op1=ALU.add).then_inc(
                        sem(f"summed{tile}"), 1)

        @block.scalar
        def _(act):
            with act.Fori(0, TURNS) as i:
                for tile in range(SETS):
                    act.wait_ge(sem(f"summed{tile}"), i + 2)
                    act.dma_start(out[0, bass.ds((SETS * i + tile) * P, P), :], x[tile][:]).then_inc(
                        sem(f"out{tile}"), 16)
            for tile in range(SETS):
                act.wait_ge(sem(f"out{tile}"), 16 * (TURNS + 1))


class Constants:
    pass


INPUTS = ["x", "mem", "norm_mix", "w_in", "shift_mu", "decay_w0", "decay_w2", "iclr_a0", "iclr_a2", "gate_g2",
          "rw_k_k", "rw_k_a", "rw_r_k", "lnx_w", "lnx_b", "att_q_norm", "att_k_norm", "att_rel_bias",
          "att_out_norm", "w_out", "norm_xa", "norm_mem", "xa_w_q", "xa_w_kv", "xa_w_o", "xa_q_norm", "xa_k_norm",
          "norm_ffn", "moe_w_group", "moe_b_group", "moe_w_route", "moe_b_route", "moe_w_gate", "moe_w_up",
          "moe_w_down"]


def build(nc, a, out):
    dram = {
        "rw": nc.dram_tensor("scratch_rw", (RW_TILES, P, SEQ), F32).ap(),
        "q": nc.dram_tensor("scratch_q", (CT, P, SEQ), F32).ap(),
        "k": nc.dram_tensor("scratch_k", (CT, P, PREV + SEQ), F32).ap(),
        "v": nc.dram_tensor("scratch_v", (PREV + SEQ, RW), F32).ap(),
        "x3": nc.dram_tensor("scratch_x3", (SEQ, DM), F32).ap(),
        "h_ffn": nc.dram_tensor("scratch_h_ffn", (SEQ, DM), F32).ap(),
        "bias": nc.dram_tensor("scratch_bias", (P, HEADS, BAND), F32).ap(),
        "slot_token": nc.dram_tensor("scratch_slot_token", (SLOTS, 1), I32).ap(),
        "y": nc.dram_tensor("scratch_y", (SLOTS, DM), F32).ap(),
    }
    with ExitStack() as stack:
        sb = Memory(nc, stack, "constant")
        c = Constants()
        c.eps = sb("eps", P, 1)
        c.lnx_eps = sb("lnx_eps", P, 1)
        c.ones = sb("ones", P, 1)
        c.ident = sb("ident", P, P)
        c.every = sb("every", P, P)
        c.ident_half = sb("ident_half", P, HD)
        c.same_head = sb("same_head", P, P)
        c.all_heads = sb("all_heads", P, CT, HEADS)
        c.head_rows = sb("head_rows", HEADS, RW)
        c.causal = sb("causal", P, P)
        c.level_mask = sb("level_mask", P, len(LEVELS), HD)
        c.level_mask_t = sb("level_mask_t", P, 1, HD)
        c.within = sb("within", P, N512)
        banks = stack.enter_context(nc.psum_tensor("banks", [P, 8, N512], F32))
        build_constants(nc, c)
        logits = sb("logits", P, TILES, LOGITS)
        with ExitStack() as mixing:
            mb = Memory(nc, mixing, "kept")
            m = Constants()
            m.logits = logits
            m.w_out, m.w_q, m.w_o = mb("w_out", P, KT, DM), mb("w_q", P, KT, XW), mb("w_o", P, XH, DM)
            with ExitStack() as projections:
                c.h_t = Memory(nc, projections, "projection")("h_t", P, KT, SEQ)
                norm_and_project_v(nc, a, c, dram, banks)
                project_rwkv(nc, a, c, dram, banks)
                project_attention(nc, a, c, m, dram, banks)
            m.bias = mb("bias", P, HEADS, BAND)
            m.state = mb("state", P, CT, HD)
            m.shift_back = mb("shift_back", HEADS, 1)
            m.lora_wa, m.gate = mb("lora_wa", P, RW), mb("gate", P, RW)
            m.k_mem, m.v_mem = mb("k_mem", P, XH, N_MEM), mb("v_mem", P, MT, XW)
            m.gain_ffn = mb("gain_ffn", P, KT)
            m.w_router, m.b_router = mb("w_router", P, KT, LOGITS), mb("b_router", P, LOGITS)
            m.w0, m.a0, m.gain_kk, m.ln_w, m.ln_b, m.gain_att, m.r_k, m.half_k_a, m.rest_k_a = (
                mb(n, P, CT) for n in ("w0", "a0", "gain_kk", "ln_w", "ln_b", "gain_att", "r_k", "half_k_a",
                                       "rest_k_a"))
            m.gain_xa, m.gain_q, m.scaled_q = mb("gain_xa", P, KT), mb("gain_q", P, 1), mb("scaled_q", P, 1)
            load_mixer(nc, a, c, m, dram, banks)
            mix_tokens(nc, a, c, m, dram, banks)
        with ExitStack() as routing:
            rb = Memory(nc, routing, "routing")
            r = Constants()
            r.logits = logits
            r.slot_of = rb("slot_of", P, TILES, 2, dt=I32)
            r.weight = rb("weight", P, TILES, 2)
            r.expert_of = rb("expert_of", 1, BLOCKS, dt=I32)
            r.turns = rb("turns", 1, 1, dt=I32)
            r.gain = rb("gain", P, KT)
            route_tokens(nc, a, c, r, dram, banks)
            run_experts(nc, a, c, r, dram, banks)
            combine_experts(nc, r, dram, out)


def kernel(**inputs):
    from concourse import bacc
    from concourse.bass_utils import run_bass_kernel_spmd

    nc = bacc.Bacc("TRN2", target_bir_lowering=False, num_devices=1)
    arrays, args = {}, {}
    for name in INPUTS:
        value = np.asarray(inputs[name])
        if name == "att_rel_bias":
            distance = np.arange(P)[:, None] + PREV - np.arange(BAND)[None, :]
            index = np.clip(distance, -(CHUNK - 1), REL_MAX) + CHUNK - 1
            value = value[0][:, index].transpose(1, 0, 2)
        value = np.ascontiguousarray(value)
        arrays[f"in_{name}"] = value
        args[name] = nc.dram_tensor(f"in_{name}", value.shape, mybir.dt.from_np(value.dtype),
                                    kind="ExternalInput").ap()
    out = nc.dram_tensor("out", (1, SEQ, DM), F32, kind="ExternalOutput").ap()
    build(nc, args, out)
    result = run_bass_kernel_spmd(nc, [arrays], core_ids=[0])
    return result.results[0]["out"]
```
